# Optimizing a Trainium2 kernel written in Bass

```python
import math
import jax, jax.numpy as jnp
from jax import lax
import numpy as np

D_MODEL = 2048
BATCH = 1
SEQ = 128
DEPTH = 1
DEC_BATCH = 1
DEC_SEQ = 512
PAST_LEN = 128

GRID_W = 64
N_HEADS = 12
HEAD_DIM = 128
D_ATTN = N_HEADS * HEAD_DIM
D_SSM = 512
SSM_GROUP = 16
N_GROUPS = D_SSM // SSM_GROUP
STATE_DIM = 64
D_MIX = D_ATTN + D_SSM
D_IN = 3 * D_ATTN + D_SSM
WIN_H = 8
WIN_W = 16
Q_COL_BLOCK = 16
K_COL_BLOCK = 32
N_COL_BLOCKS = GRID_W // Q_COL_BLOCK
CTX_Q_BLOCK = 128
N_EXPERTS = 16
EXPERT_FF = 1024
CAPACITY_FACTOR = 2
EPS = 1e-6
NEG_INF = -1e30

kernel_name = "hymba_natten_s5_ec_diffusion_step"

def rmsnorm(x, g):
    xf = x.astype(jnp.float32)
    y = xf * lax.rsqrt(jnp.mean(xf * xf, axis=-1, keepdims=True) + EPS)
    return (y * g.astype(jnp.float32)).astype(x.dtype)

def adaln(cond, w_ada, b_ada):
    m = jax.nn.silu(cond) @ w_ada + b_ada
    return jnp.split(m[:, None, :], 6, axis=-1)

def modulate(x, shift, scale):
    return x * (1 + scale) + shift

def mixer_inputs(h, p):
    B, L, _ = h.shape
    z = h @ p['w_in']
    q = rmsnorm(z[..., :D_ATTN].reshape(B, L, N_HEADS, HEAD_DIM), p['q_norm'])
    k = rmsnorm(z[..., D_ATTN:2 * D_ATTN].reshape(B, L, N_HEADS, HEAD_DIM), p['k_norm'])
    v = z[..., 2 * D_ATTN:3 * D_ATTN].reshape(B, L, N_HEADS, HEAD_DIM)
    u = z[..., 3 * D_ATTN:]
    return q, k, v, u

def context_attention(q, k, v):
    B, L, H, dh = q.shape
    nb = L // CTX_Q_BLOCK
    qb = jnp.moveaxis(q.reshape(B, nb, CTX_Q_BLOCK, H, dh), 1, 0)
    scale = HEAD_DIM ** -0.5

    def block(qi):
        s = jnp.einsum('bqhd,bkhd->bhqk', qi, k).astype(jnp.float32) * scale
        pr = jax.nn.softmax(s, axis=-1).astype(v.dtype)
        return jnp.einsum('bhqk,bkhd->bqhd', pr, v)

    o = lax.map(block, qb)
    return jnp.moveaxis(o, 0, 1).reshape(B, L, H * dh)

def _col_tables():
    j = np.arange(N_COL_BLOCKS)
    k_start = np.clip(j * Q_COL_BLOCK - WIN_W // 2, 0, GRID_W - K_COL_BLOCK)
    key_cols = k_start[:, None] + np.arange(K_COL_BLOCK)[None, :]
    q_cols = j[:, None] * Q_COL_BLOCK + np.arange(Q_COL_BLOCK)[None, :]
    cs = np.clip(q_cols - WIN_W // 2, 0, GRID_W - WIN_W)
    kc = key_cols[:, None, :]
    mask = (kc >= cs[..., None]) & (kc < cs[..., None] + WIN_W)
    dc_idx = np.clip(kc - q_cols[..., None], -(WIN_W - 1), WIN_W - 1) + (WIN_W - 1)
    return key_cols, mask, dc_idx

def neighbourhood_attention(q, k, v, k_ctx, v_ctx, rpb):
    B, L, H, dh = q.shape
    rows = L // GRID_W
    kh = min(WIN_H, rows)
    key_cols, col_mask, dc_idx = _col_tables()
    qg = q.reshape(B, rows, N_COL_BLOCKS, Q_COL_BLOCK, H, dh)
    kg = k.reshape(B, rows, GRID_W, H, dh)
    vg = v.reshape(B, rows, GRID_W, H, dh)
    rpb_cols = rpb[:, :, dc_idx]
    mask = jnp.asarray(col_mask)[:, :, None, :]
    scale = HEAD_DIM ** -0.5
    n_loc = kh * K_COL_BLOCK

    def row_block(r):
        rs = jnp.clip(r - kh // 2, 0, rows - kh)
        kr = lax.dynamic_slice_in_dim(kg, rs, kh, axis=1)[:, :, key_cols]
        vr = lax.dynamic_slice_in_dim(vg, rs, kh, axis=1)[:, :, key_cols]
        qr = lax.dynamic_index_in_dim(qg, r, axis=1, keepdims=False)
        s_loc = jnp.einsum('bjqhd,bijkhd->bhjqik', qr, kr).astype(jnp.float32) * scale
        dr_idx = rs + jnp.arange(kh) - r + (WIN_H - 1)
        bias = jnp.transpose(rpb_cols[:, dr_idx], (0, 2, 3, 1, 4))
        s_loc = jnp.where(mask, s_loc + bias.astype(jnp.float32), NEG_INF)
        s_loc = s_loc.reshape(B, H, N_COL_BLOCKS, Q_COL_BLOCK, n_loc)
        s_ctx = jnp.einsum('bjqhd,bkhd->bhjqk', qr, k_ctx).astype(jnp.float32) * scale
        pr = jax.nn.softmax(jnp.concatenate([s_loc, s_ctx], axis=-1), axis=-1).astype(v.dtype)
        p_loc = pr[..., :n_loc].reshape(B, H, N_COL_BLOCKS, Q_COL_BLOCK, kh, K_COL_BLOCK)
        o = (jnp.einsum('bhjqik,bijkhd->bjqhd', p_loc, vr)
             + jnp.einsum('bhjqk,bkhd->bjqhd', pr[..., n_loc:], v_ctx))
        return o.reshape(B, GRID_W, H * dh)

    o = lax.map(row_block, jnp.arange(rows))
    return jnp.moveaxis(o, 0, 1).reshape(B, L, H * dh)

def ssm_discretize(p):
    a = lax.complex(p['ssm_a_re'].astype(jnp.float32), p['ssm_a_im'].astype(jnp.float32))
    dt = jnp.exp(p['ssm_log_dt'].astype(jnp.float32))[..., None]
    a_bar = jnp.exp(a * dt)
    b = lax.complex(p['ssm_b_re'].astype(jnp.float32), p['ssm_b_im'].astype(jnp.float32))
    b_bar = ((a_bar - 1) / a)[..., None] * b
    return a_bar, b_bar

def _ssm_combine(e1, e2):
    a1, b1 = e1
    a2, b2 = e2
    return a1 * a2, a2 * b1 + b2

def ssm_scan(uc, a_bar, b_bar, reverse):
    bu = jnp.einsum('blgc,gpc->blgp', uc, b_bar)
    a = jnp.broadcast_to(a_bar[None, None], (1, uc.shape[1]) + a_bar.shape)
    return lax.associative_scan(_ssm_combine, (a, bu), axis=1, reverse=reverse)

def s5_states(u, p, h0):
    B, L, _ = u.shape
    a_bar, b_bar = ssm_discretize(p)
    uc = u.astype(jnp.float32).reshape(B, L, N_GROUPS, SSM_GROUP).astype(jnp.complex64)
    hs = []
    for direction in range(2):
        a_cum, h = ssm_scan(uc, a_bar[direction], b_bar[direction], reverse=(direction == 1))
        if h0 is not None:
            h = h + a_cum * h0[:, direction][:, None]
        hs.append(h)
    return hs

def s5_readout(hs, u, p):
    B, L, _ = u.shape
    c = lax.complex(p['ssm_c_re'].astype(jnp.float32), p['ssm_c_im'].astype(jnp.float32))
    uf = u.astype(jnp.float32)
    y = p['ssm_d'].astype(jnp.float32) * uf
    for direction in range(2):
        y = y + jnp.einsum('blgp,gcp->blgc', hs[direction], c[direction]).real.reshape(B, L, D_SSM)
    g = jax.nn.gelu(y)
    out = g * jax.nn.sigmoid(g @ p['w_glu'].astype(jnp.float32) + p['b_glu'].astype(jnp.float32))
    return out.astype(u.dtype)

def expert_choice_ffn(x, p):
    B, L, D = x.shape
    cap = CAPACITY_FACTOR * L // N_EXPERTS
    aff = jax.nn.softmax((x @ p['w_router']).astype(jnp.float32), axis=-1)
    g, idx = lax.top_k(jnp.swapaxes(aff, 1, 2), cap)
    bidx = jnp.arange(B)[:, None, None]
    xs = x[bidx, idx]
    h = (jax.nn.silu(jnp.einsum('becd,edf->becf', xs, p['w_gate']))
         * jnp.einsum('becd,edf->becf', xs, p['w_up']))
    y = jnp.einsum('becf,efd->becd', h, p['w_down']) * g[..., None].astype(x.dtype)
    return jnp.zeros_like(x).at[bidx, idx].add(y)

def context_layer(x, mod, p):
    sh1, sc1, g1, sh2, sc2, g2 = mod
    h = modulate(rmsnorm(x, p['norm1']), sh1, sc1)
    q, k, v, u = mixer_inputs(h, p)
    attn = context_attention(q, k, v)
    hs = s5_states(u, p, None)
    finals = jnp.stack([hs[0][:, -1], hs[1][:, 0]], axis=1)
    ssm = s5_readout(hs, u, p)
    x = x + g1 * (jnp.concatenate([attn, ssm], axis=-1) @ p['w_out'])
    h = modulate(rmsnorm(x, p['norm2']), sh2, sc2)
    x = x + g2 * expert_choice_ffn(h, p)
    return x, k, v, finals

def latent_layer(x, mod, k_ctx, v_ctx, h0, p):
    sh1, sc1, g1, sh2, sc2, g2 = mod
    h = modulate(rmsnorm(x, p['norm1']), sh1, sc1)
    q, k, v, u = mixer_inputs(h, p)
    attn = neighbourhood_attention(q, k, v, k_ctx, v_ctx, p['rpb'])
    ssm = s5_readout(s5_states(u, p, h0), u, p)
    x = x + g1 * (jnp.concatenate([attn, ssm], axis=-1) @ p['w_out'])
    h = modulate(rmsnorm(x, p['norm2']), sh2, sc2)
    x = x + g2 * expert_choice_ffn(h, p)
    return x

def setup_inputs(seed: int = 0) -> dict:
    key = jax.random.key(seed)
    ks = jax.random.split(key, 32)
    f32 = jnp.float32

    def nrm(k, shape, s):
        return jax.random.normal(k, shape, f32) * s

    G, P = N_GROUPS, STATE_DIM
    n = jnp.arange(P, dtype=f32)
    return {
        "x_prompt": nrm(ks[0], (BATCH, SEQ, D_MODEL), 1.0),
        "x_sample": nrm(ks[1], (DEC_BATCH, DEC_SEQ, D_MODEL), 1.0),
        "cache_k": nrm(ks[2], (DEC_BATCH, DEPTH, PAST_LEN, N_HEADS, HEAD_DIM), 1.0),
        "cache_v": nrm(ks[3], (DEC_BATCH, DEPTH, PAST_LEN, N_HEADS, HEAD_DIM), 1.0),
        "state_ssm_re": nrm(ks[4], (DEC_BATCH, DEPTH, 2, G, P), 0.5),
        "state_ssm_im": nrm(ks[5], (DEC_BATCH, DEPTH, 2, G, P), 0.5),
        "c": nrm(ks[6], (DEC_BATCH, D_MODEL), 1.0),
        "c_ctx": nrm(ks[7], (D_MODEL,), 1.0),
        "w_ada": nrm(ks[8], (DEPTH, D_MODEL, 6 * D_MODEL), 0.5 * D_MODEL ** -0.5),
        "b_ada": nrm(ks[9], (DEPTH, 6 * D_MODEL), 0.02),
        "norm1_g": 1.0 + nrm(ks[10], (DEPTH, D_MODEL), 0.02),
        "norm2_g": 1.0 + nrm(ks[11], (DEPTH, D_MODEL), 0.02),
        "w_in": nrm(ks[12], (DEPTH, D_MODEL, D_IN), D_MODEL ** -0.5),
        "q_norm_g": 1.0 + nrm(ks[13], (DEPTH, HEAD_DIM), 0.02),
        "k_norm_g": 1.0 + nrm(ks[14], (DEPTH, HEAD_DIM), 0.02),
        "rel_pos_bias": nrm(ks[15], (DEPTH, N_HEADS, 2 * WIN_H - 1, 2 * WIN_W - 1), 0.5),
        "ssm_a_re": -0.5 + nrm(ks[16], (DEPTH, 2, G, P), 0.01),
        "ssm_a_im": math.pi * n + nrm(ks[17], (DEPTH, 2, G, P), 0.01),
        "ssm_log_dt": jax.random.uniform(ks[18], (DEPTH, 2, G), f32, math.log(0.001), math.log(0.1)),
        "ssm_b_re": nrm(ks[19], (DEPTH, 2, G, P, SSM_GROUP), SSM_GROUP ** -0.5),
        "ssm_b_im": nrm(ks[20], (DEPTH, 2, G, P, SSM_GROUP), SSM_GROUP ** -0.5),
        "ssm_c_re": nrm(ks[21], (DEPTH, 2, G, SSM_GROUP, P), P ** -0.5),
        "ssm_c_im": nrm(ks[22], (DEPTH, 2, G, SSM_GROUP, P), P ** -0.5),
        "ssm_d": nrm(ks[23], (DEPTH, D_SSM), 0.5),
        "w_glu": nrm(ks[24], (DEPTH, D_SSM, D_SSM), D_SSM ** -0.5),
        "b_glu": nrm(ks[25], (DEPTH, D_SSM), 0.02),
        "w_out": nrm(ks[26], (DEPTH, D_MIX, D_MODEL), D_MIX ** -0.5),
        "w_router": nrm(ks[27], (DEPTH, D_MODEL, N_EXPERTS), D_MODEL ** -0.5),
        "w_expert_gate": nrm(ks[28], (DEPTH, N_EXPERTS, D_MODEL, EXPERT_FF), D_MODEL ** -0.5),
        "w_expert_up": nrm(ks[29], (DEPTH, N_EXPERTS, D_MODEL, EXPERT_FF), D_MODEL ** -0.5),
        "w_expert_down": nrm(ks[30], (DEPTH, N_EXPERTS, EXPERT_FF, D_MODEL), EXPERT_FF ** -0.5),
    }

def reference(x_prompt, x_sample, cache_k, cache_v, state_ssm_re, state_ssm_im, c, c_ctx,
              w_ada, b_ada, norm1_g, norm2_g, w_in, q_norm_g, k_norm_g, rel_pos_bias,
              ssm_a_re, ssm_a_im, ssm_log_dt, ssm_b_re, ssm_b_im, ssm_c_re, ssm_c_im,
              ssm_d, w_glu, b_glu, w_out, w_router, w_expert_gate, w_expert_up, w_expert_down):
    xp = x_prompt
    xs = x_sample
    ks_out, vs_out, hre_out, him_out = [], [], [], []
    for l in range(DEPTH):
        p = dict(norm1=norm1_g[l], norm2=norm2_g[l], w_in=w_in[l], q_norm=q_norm_g[l],
                 k_norm=k_norm_g[l], rpb=rel_pos_bias[l], ssm_a_re=ssm_a_re[l],
                 ssm_a_im=ssm_a_im[l], ssm_log_dt=ssm_log_dt[l], ssm_b_re=ssm_b_re[l],
                 ssm_b_im=ssm_b_im[l], ssm_c_re=ssm_c_re[l], ssm_c_im=ssm_c_im[l],
                 ssm_d=ssm_d[l], w_glu=w_glu[l], b_glu=b_glu[l], w_out=w_out[l],
                 w_router=w_router[l], w_gate=w_expert_gate[l], w_up=w_expert_up[l],
                 w_down=w_expert_down[l])
        mod_ctx = adaln(c_ctx[None, :], w_ada[l], b_ada[l])
        mod_lat = adaln(c, w_ada[l], b_ada[l])
        xp, k_l, v_l, h_l = context_layer(xp, mod_ctx, p)
        ks_out.append(k_l)
        vs_out.append(v_l)
        hre_out.append(jnp.real(h_l))
        him_out.append(jnp.imag(h_l))
        h0 = lax.complex(state_ssm_re[:, l].astype(jnp.float32), state_ssm_im[:, l].astype(jnp.float32))
        xs = latent_layer(xs, mod_lat, cache_k[:, l], cache_v[:, l], h0, p)
    new_cache_k = jnp.stack(ks_out, axis=1)
    new_cache_v = jnp.stack(vs_out, axis=1)
    new_state_re = jnp.stack(hre_out, axis=1)
    new_state_im = jnp.stack(him_out, axis=1)
    return (xp, xs, new_cache_k, new_cache_v, new_state_re, new_state_im)


_drawn_inputs = setup_inputs


def setup_inputs(seed=0):
    import zlib

    import numpy as np

    out = dict(_drawn_inputs(seed))
    spreads = {}
    factors = {'cache_k': 3.801,
     'cache_v': 3.13,
     'state_ssm_re': 3.573,
     'state_ssm_im': 3.532,
     'norm1_g': 2.946,
     'norm2_g': 7.852,
     'q_norm_g': 8.0,
     'k_norm_g': 2.847,
     'rel_pos_bias': 5.431,
     'ssm_a_re': 19.059,
     'ssm_c_re': 3.299,
     'ssm_c_im': 3.23,
     'w_glu': 6.728,
     'b_glu': 52.402}
    for name, (base, spread) in spreads.items():
        noise = np.random.default_rng([zlib.crc32(name.encode()), seed]).standard_normal(out[name].shape)
        drawn = base * np.exp(spread * noise) if base else spread * noise
        out[name] = __import__('jax').numpy.asarray(drawn.astype(out[name].dtype))
    for name, factor in factors.items():
        out[name] = (out[name] * factor).astype(out[name].dtype)
    return out
```

```python
from contextlib import ExitStack, contextmanager
import math

import numpy as np
import concourse.bass as bass
from concourse import mybir

F32 = mybir.dt.float32
U32 = mybir.dt.uint32
ALU = mybir.AluOpType
ACT = mybir.ActivationFunctionType
AX = mybir.AxisListType.X

P = 128
D = 2048
KT = D // P
N_CTX = 128
N_LAT = 512
TOK = N_CTX + N_LAT
TT = TOK // P
GRID_W = 64
ROWS = N_LAT // GRID_W
HEADS = 12
HD = 128
D_ATTN = HEADS * HD
D_SSM = 512
STATE = 64
SSM_C = 16
MIX_T = (D_ATTN + D_SSM) // P
CHUNKS_M = D_SSM // P
QS = 4
EXPERTS = 16
FF = 1024
CAP_L = 2 * N_LAT // EXPERTS
CAP_C = 2 * N_CTX // EXPERTS
SLOTS = CAP_L + CAP_C
EPS = 1e-6
NEG = -1e30
RPB_W = 31
RPB_H = 15
SPAN = 7 * RPB_W + 32 + 16
RPB_PAD = 16
SEG = 32
NSEG = N_LAT // SEG
BANK = 512
ADA_MIX = 2 * D // BANK
assert ADA_MIX // 2 == TT - 1, "a tile of x after every two pieces"
ADA_LATE = 4 * D // (8 * CHUNKS_M)
KEY_START = [0, 64, 192, 256]
VARIANT = [0, 1, 1, 2]
BIAS_OFF = [16, 8, 0]
START = 12


class Chain:

    def __init__(self, eng, sem):
        self.eng, self.sem, self.base, self.k = eng, sem, 0, 0

    def mark(self, ins):
        ins.then_inc(self.sem, 1)
        self.k += 1

    def wait(self):
        self.eng.wait_ge(self.sem, self.base + self.k)

    def link(self, ins):
        self.mark(ins)
        self.wait()

    @contextmanager
    def body(self, i, per):
        start, self.base, self.k = self.base + self.k, self.base + self.k + i * per, 0
        yield
        assert self.k == per, (self.k, per)
        self.base, self.k = start, 0

    def passed(self, n):
        self.base = self.base + n


def trunk_step(nc, t, out):
    ctx = ExitStack()
    with ctx:
        def sb(name, shape, dt=F32):
            return ctx.enter_context(nc.sbuf_tensor(name, shape, dt))

        free = []

        def sem(name):
            return ctx.enter_context(nc.semaphore(name))

        def free_sem(name, start=START):
            s = sem(name)
            free.append((s, start))
            return s

        def apart(eng):
            eng.sem_inc(s_steps, 1)

        mod_d = nc.dram_tensor("mod_rows", (2, 6 * D), F32, kind="Internal").ap()
        h2_d = nc.dram_tensor("h2_rows", (TOK, D), F32, kind="Internal").ap()

        PS = ctx.enter_context(nc.psum_tensor("PS", [P, 8 * BANK], F32))

        def bank(b, n=BANK, at=0):
            return PS[:, b * BANK + at:b * BANK + at + n]

        consts = sb("consts", [P, 352])
        ident, ones = consts[:, 0:128], consts[:, 128:256]
        masks = consts[:, 256:352].rearrange("p (v k) -> p v k", v=3)
        hT_ = sb("hT_", [P, KT * TOK])
        hT = hT_[:, :].rearrange("p (k t) -> p k t", k=KT)
        mixT_ = sb("mixT_", [P, MIX_T * TOK])
        mixT = mixT_[:, :].rearrange("p (k t) -> p k t", k=MIX_T)
        gT = mixT_[:, 0:4 * TOK].rearrange("p (k t) -> p k t", k=4)
        pcol = sb("pcol", [P, 26])
        b_glu_c, ssm_d_c, norm1_c = pcol[:, 0:4], pcol[:, 4:8], pcol[:, 8:24]
        q_gain_raw, k_gain = pcol[:, 24:25], pcol[:, 25:26]
        q_gain = sb("q_gain", [P, 1])
        eps = sb("eps", [P, 1])
        cT = sb("cT", [P, 32])
        cTv = cT[:, :].rearrange("p (c k) -> p c k", c=2)
        lane = sb("lane", [P, 7 * 32])
        lanev = lane[:, :].rearrange("p (n t) -> p n t", n=7)
        fin = sb("fin", [P, 64])
        scale1 = sb("scale1", [P, 32])
        shift1 = sb("shift1", [P, 32])
        small = sb("small", [P, 64])
        work = sb("work", [P, 31880])
        used = [0]

        def at(start):
            used[0] = start

        def take(n, parts=P):
            a = used[0]
            used[0] += n
            assert used[0] <= 31880, used[0]
            return work[0:parts, a:a + n]

        at(0)
        E2 = take(2048).rearrange("p (c t s) -> p c t s", c=2, t=32)
        E1 = take(1024).rearrange("p (c t s) -> p c t s", c=2, t=32)
        BT = take(2048).rearrange("p (m d c l) -> p m (d c l)", m=4, d=2, c=2)
        CT = take(3072).rearrange("p (m d c l) -> p m d c l", m=4, d=2, c=3)
        after_tables = used[0]
        w_ada_ring = [take(8192).rearrange("p (k n) -> p k n", k=KT) for _ in range(2)]
        b_ada_ring = [take(512, 2) for _ in range(2)]
        mod_ring = [take(512, 2) for _ in range(2)]
        prow = take(128, 26)
        crow = take(128, 32)
        modrow = take(128, 64)
        ldt = take(2, 32)
        r_are, r_aim, r_h0r, r_h0i = [take(128, 32) for _ in range(4)]
        r_tmp = [take(128, 32) for _ in range(14)]
        cexp = take(2048).rearrange("p (c n) -> p c n", c=2)
        x_in = mixT_[:, 0:D]
        x_n = mixT_[:, D:2 * D]
        bexp = mixT_[:, 4096:4096 + 2048].rearrange("p (c n) -> p c n", c=2)
        bbar = mixT_[:, 6144:6144 + 2048].rearrange("p (c n) -> p c n", c=2)
        bscr = mixT_[:, 8192:8192 + 2048].rearrange("p (c n) -> p c n", c=2)

        at(after_tables)
        w_u = take(2048).rearrange("p (k n) -> p k n", k=KT)
        uT = take(2 * TOK).rearrange("p (d t) -> p d t", d=2)
        BTm = take(512).rearrange("p (d c l) -> p d c l", d=2, c=2)
        CTm = take(768).rearrange("p (d c l) -> p d c l", d=2, c=3)
        E2m = take(512).rearrange("p (c d q s) -> p c d q s", c=2, d=2, q=4)
        E1m = take(256).rearrange("p (c d q s) -> p c d q s", c=2, d=2, q=4)
        lanem = take(24).rearrange("p (n d q) -> p n d q", n=3, d=2)
        finm = take(16).rearrange("p (c d q) -> p c d q", c=2, d=2)
        rot = [take(2 * TOK).rearrange("p (c t) -> p c t", c=2) for _ in range(3)]
        rot_tmp = take(2 * N_LAT).rearrange("p (c t) -> p c t", c=2)
        prod = [take(4 * TOK).rearrange("p (c t) -> p c t", c=4) for _ in range(2)]
        rin = take(2 * TOK).rearrange("p (c t) -> p c t", c=2)
        gsc = take(2 * TOK).rearrange("p (c t) -> p c t", c=2)
        back = mixT_[:, 4 * TOK:8 * TOK].rearrange("p (c t) -> p c t", c=4)
        y_u = mixT_[:, 8 * TOK:9 * TOK]
        fin_rows = [take(128, 32) for _ in range(2)]
        b_late = [take(ADA_LATE, 1) for _ in range(2)]
        row_late = [take(ADA_LATE, 2) for _ in range(2)]
        before_late = used[0]
        w_late = [x.rearrange("p (k n) -> p k n", k=KT)
                  for x in (mixT_[:, 9 * TOK:9 * TOK + KT * ADA_LATE], take(KT * ADA_LATE))]
        at(before_late)
        w_glu = take(2048).rearrange("p (k n) -> p k n", k=4)
        sig_u = [take(TOK) for _ in range(2)]

        at(0)
        w_qkv = [take(6144).rearrange("p (k c n) -> p k c n", k=KT, c=3) for _ in range(2)]
        spans = take(HEADS * SPAN).rearrange("p (h s) -> p h s", h=HEADS)
        span = take(SPAN)
        rstd = take(TOK)
        at(max(used[0], 2 * 8192))
        biasm = [take(768).rearrange("p (v n) -> p v n", v=3) for _ in range(2)]
        qT = [take(TOK) for _ in range(2)]
        kT = [take(TOK) for _ in range(2)]
        vS = [take(TOK).rearrange("p (t n) -> p t n", t=TT) for _ in range(2)]
        sq = [take(TOK) for _ in range(2)]
        kc_in = [take(128) for _ in range(2)]
        kcT = [take(128) for _ in range(2)]
        vc = [take(128) for _ in range(2)]
        knat = [take(128) for _ in range(2)]
        probs = [take(448) for _ in range(2)]
        probsT = take(3 * P)
        probsT_half = take(2 * P)
        attention_end = used[0]

        at(0)
        w_out_ring = [take(8192).rearrange("p (k n) -> p k n", k=MIX_T) for _ in range(2)]
        x1 = hT_[:, :].rearrange("p (t d) -> p t d", t=TT)
        scale2 = take(2 * D).rearrange("p (c n) -> p c n", c=2)
        shift2 = take(2 * D).rearrange("p (c n) -> p c n", c=2)
        norm2 = take(D)
        w_r = take(256).rearrange("p (k e) -> p k e", k=KT)
        aff = take(TT * 16).rearrange("p (t e) -> p t e", t=TT)
        stat = take(40).rearrange("p (t n) -> p t n", t=TT)
        affT = take(TOK, 16)
        top_v = take(SLOTS, 16)
        top_i = take(SLOTS, 16).bitcast(U32)
        top_a = take(2 * SLOTS, 16).bitcast(U32)
        top_f = take(SLOTS, 16)
        assert used[0] >= attention_end, "what follows is used while attention still runs"
        gate1 = [take(1024).rearrange("p (c n) -> p c n", c=2) for _ in range(2)]
        gated = [take(512) for _ in range(2)]
        h2 = [mixT_[:, i * D:(i + 1) * D] for i in range(2)]
        h2T = [mixT_[:, (2 + i) * D:(3 + i) * D].rearrange("p (k t) -> p k t", k=KT) for i in range(2)]
        junk = take(BANK)
        ssq = take(TT * 4).rearrange("p (t n) -> p t n", t=TT)
        slot_gate = take(16, SLOTS)
        slot_row = take(16, SLOTS).bitcast(U32)
        row_now = [take(1, SLOTS).bitcast(U32) for _ in range(2)]

        at(0)
        RING = 3
        w_ring = [take(8192) for _ in range(RING)]
        gate2 = mixT_[0:SLOTS, 0:D]
        xs = [mixT_[0:SLOTS, D * (1 + i):D * (2 + i)] for i in range(2)]
        y_e = [mixT_[0:SLOTS, D * (3 + i):D * (4 + i)] for i in range(2)]
        xsT = [hT_[:, i * 1280:(i + 1) * 1280].rearrange("p (k s) -> p k s", k=KT) for i in range(2)]
        act_g = hT_[0:SLOTS, 2560:2560 + FF]
        act_h = hT_[0:SLOTS, 3584:3584 + FF]
        actT = hT_[:, 4608:4608 + 8 * SLOTS].rearrange("p (k s) -> p k s", k=8)

        s_eps = sem("s_eps")
        s_xsum = sem("s_xsum")
        s_root = free_sem("s_root")
        s_ssum = sem("s_ssum")
        s_nroot = sem("s_nroot")
        s_steps = sem("s_steps")
        s_const = sem("s_const")
        s_small = sem("s_small")
        s_bzero = sem("s_bzero")
        s_bload = sem("s_bload")
        s_x = sem("s_x")
        s_xn = free_sem("s_xn")
        s_xt = free_sem("s_xt")
        s_xev = free_sem("s_xev")
        s_pt = sem("s_pt")
        s_pcol = sem("s_pcol")
        s_ct = sem("s_ct")
        s_ada = [sem(f"s_ada{i}") for i in range(2)]
        s_ada_mm = free_sem("s_ada_mm")
        s_mod = free_sem("s_mod")
        s_modout = [free_sem(f"s_modout{i}", 16) for i in range(2)]
        s_modrow = sem("s_modrow")
        s_modT = sem("s_modT")
        s_mods = sem("s_mods")
        s_hlat = sem("s_hlat")
        s_hctx = sem("s_hctx")
        s_rows = sem("s_rows")
        s_ract = sem("s_ract")
        s_rdve = sem("s_rdve")
        s_lane = sem("s_lane")
        s_tab = sem("s_tab")
        s_bbar = sem("s_bbar")
        s_bct = sem("s_bct")
        s_bcev = sem("s_bcev")
        s_wu = sem("s_wu")
        s_late = [sem(f"s_late{i}") for i in range(2)]
        s_late_mm = free_sem("s_late_mm")
        s_late_row = free_sem("s_late_row")
        s_late_out = [free_sem(f"s_late_out{i}", 16) for i in range(2)]
        s_u = free_sem("s_u")
        s_uev = free_sem("s_uev")
        s_urev = sem("s_urev")
        s_smcopy = sem("s_smcopy")
        s_bu = sem("s_bu")
        s_rmul = free_sem("s_rmul")
        s_table = sem("s_table")
        s_rot = sem("s_rot")
        s_radd = sem("s_radd")
        s_scan = free_sem("s_scan")
        s_back = free_sem("s_back")
        s_backp = free_sem("s_backp")
        s_y = free_sem("s_y")
        s_yu = free_sem("s_yu")
        s_g = free_sem("s_g")
        s_finT = sem("s_finT")
        s_finout = sem("s_finout")
        s_wglu = sem("s_wglu")
        s_glu = sem("s_glu")
        s_sig = sem("s_sig")
        s_mixu = sem("s_mixu")

        s_span = sem("s_span")
        s_padz = sem("s_padz")
        s_wqkv = [sem(f"s_wqkv{i}") for i in range(2)]
        s_cache = [sem(f"s_cache{i}") for i in range(2)]
        s_biasm = free_sem("s_biasm")
        s_qmm = sem("s_qmm")
        s_kmm = sem("s_kmm")
        s_vmm = free_sem("s_vmm")
        s_sq = free_sem("s_sq")
        s_ss = free_sem("s_ss")
        s_qn = sem("s_qn")
        s_kn = free_sem("s_kn")
        s_vev = free_sem("s_vev")
        s_kcT = free_sem("s_kcT")
        s_kcev = free_sem("s_kcev")
        s_knT = sem("s_knT")
        s_knev = free_sem("s_knev")
        s_kvout = [free_sem(f"s_kvout{i}", 32) for i in range(2)]
        s_sc = sem("s_sc")
        s_mx = free_sem("s_mx")
        s_ex = free_sem("s_ex")
        s_pn = sem("s_pn")
        s_pT = free_sem("s_pT")
        s_pTev = free_sem("s_pTev")
        s_pv = free_sem("s_pv")
        s_o = free_sem("s_o")

        s_wout = [sem(f"s_wout{i}") for i in range(2)]
        s_g1 = [sem(f"s_g1{i}") for i in range(2)]
        s_xre = sem("s_xre")
        s_omm = free_sem("s_omm")
        s_x1 = free_sem("s_x1")
        s_n2load = sem("s_n2load")
        s_n2rows = sem("s_n2rows")
        s_ss2 = free_sem("s_ss2")
        s_h2 = sem("s_h2")
        s_x1out = sem("s_x1out")
        s_h2out = [sem(f"s_h2out{i}") for i in range(2)]
        s_h2T = sem("s_h2T")
        s_h2Tev = sem("s_h2Tev")
        s_logit = sem("s_logit")
        s_nmx = sem("s_nmx")
        s_eaff = sem("s_eaff")
        s_aff = sem("s_aff")
        s_affT = sem("s_affT")
        s_top = sem("s_top")
        s_topT = sem("s_topT")
        s_slot = sem("s_slot")
        s_gate2 = sem("s_gate2")

        s_w = [sem(f"s_w{i}") for i in range(RING)]
        s_row = sem("s_row")
        s_gath = [sem(f"s_gath{i}") for i in range(2)]
        s_xsT = sem("s_xsT")
        s_xsev = sem("s_xsev")
        s_gu = free_sem("s_gu")
        s_sg = sem("s_sg")
        s_hh = free_sem("s_hh")
        s_hhT = free_sem("s_hhT")
        s_hhev = sem("s_hhev")
        s_dn = free_sem("s_dn")
        s_ye = free_sem("s_ye")
        s_scat = sem("s_scat")
        s_added = free_sem("s_added")

        s_cload = sem("s_cload")
        s_xss = sem("s_xss")
        s_finm = free_sem("s_finm")
        s_fin = sem("s_fin")
        s_dve = sem("s_dve")
        s_pool = sem("s_pool")
        s_biased = sem("s_biased")
        s_rsum = sem("s_rsum")
        s_rstd = sem("s_rstd")
        s_h2m = sem("s_h2m")

        y_out, new_k, new_v, st_re, st_im = (out[n] for n in ("y", "new_k", "new_v", "st_re", "st_im"))
        w_in_v = t["w_in"].rearrange("(k p) n -> p k n", p=P)
        w_ada_v = t["w_ada"].rearrange("(k p) n -> p k n", p=P)
        w_out_v = t["w_out"].rearrange("(k p) n -> p k n", p=P)
        w_gate_v = t["w_gate"].rearrange("e (k p) n -> p e k n", p=P)
        w_up_v = t["w_up"].rearrange("e (k p) n -> p e k n", p=P)
        w_down_v = t["w_down"].rearrange("e (k p) n -> p e k n", p=P)

        def windows(a):
            if a == 4:
                return [(64, TT - 1, 0, P)]
            first = KEY_START[a]
            if first % P == 0:
                local = [(64, first // P, 0, P), (64 + P, first // P + 1, 0, P)]
            else:
                return [(0, first // P, 64, P), (P, first // P + 1, 0, P), (64 + 256, None, 0, P),
                        (2 * P, first // P + 2, 0, 64)]
            return local + [(64 + 256, None, 0, P)]

        def more_heads(g):
            return not isinstance(g, int) or g < HEADS - 1

        def heads_in_turn(eng, step):
            step(0, 0, 0, None)
            with eng.Fori(0, HEADS // 2 - 1) as i:
                step(2 * i + 1, 1, i, 2 * i)
                step(2 * i + 2, 0, i + 1, 2 * i + 1)
            step(HEADS - 1, 1, HEADS // 2 - 1, HEADS - 2)
            step(None, 0, None, HEADS - 1)

        block = ctx.enter_context(nc.Block())

        @block.sync
        def _(sp):
            for s, n in free:
                sp.sem_inc(s, n)
            sp.dma_start(consts[:, :], t["consts"]).then_inc(s_const, 16)
            with sp.Fori(0, ADA_MIX // 2) as i:
                for s in range(2):
                    n = 2 * i + s
                    sp.wait_ge(s_ada_mm, START + n - 1)
                    apart(sp)
                    sp.wait_ge(s_mod, START + n - 1)
                    apart(sp)
                    sp.dma_start(w_ada_ring[s], w_ada_v[:, :, bass.ds(n * BANK, BANK)]).then_inc(s_ada[s], 16)
                    sp.dma_start(b_ada_ring[s], t["b_ada"][:, bass.ds(n * BANK, BANK)].to_broadcast([2, BANK]))\
                        .then_inc(s_ada[s], 16)
            for s in range(2):
                sp.wait_ge(s_modout[s], 16 + 16 * (ADA_MIX // 2))
            for c in range(2):
                sp.dma_start(modrow[c * 32:(c + 1) * 32, :], mod_d[c, 0:2 * D].rearrange("(r n) -> r n", n=P))\
                    .then_inc(s_modrow, 16)
            sp.wait_ge(s_bct, 8)
            sp.wait_ge(s_modT, 1)
            sp.wait_ge(s_tab, 1)
            with sp.Fori(0, CHUNKS_M) as m:
                sp.wait_ge(s_u, START + m)
                apart(sp)
                sp.dma_start(w_u, w_in_v[:, :, bass.ds(m * P + 3 * D_ATTN, P)]).then_inc(s_wu, 16)
                for j in range(8):
                    sp.wait_ge(s_late_mm, START + 8 * m + j - 1)
                    apart(sp)
                    cols = bass.ds(m * (8 * ADA_LATE) + (2 * D + j * ADA_LATE), ADA_LATE)
                    sp.dma_start(w_late[j % 2], w_ada_v[:, :, cols]).then_inc(s_late[j % 2], 16)
                    sp.dma_start(b_late[j % 2], t["b_ada"][:, cols]).then_inc(s_late[j % 2], 16)
            sp.wait_ge(s_late_mm, START + 8 * CHUNKS_M)
            sp.dma_start(w_glu, t["w_glu"].rearrange("(k p) n -> p k n", p=P)).then_inc(s_wglu, 16)
            def head_weights(h, s):
                for j in range(3):
                    sp.dma_start(w_qkv[s][:, :, j, :], w_in_v[:, :, bass.ds(h * P + j * D_ATTN, P)])\
                        .then_inc(s_wqkv[s], 16)

            def head_cache(h, s):
                sp.dma_start(kc_in[s], t["cache_k"][:, bass.ds(h * P, P)]).then_inc(s_cache[s], 16)
                sp.dma_start(vc[s], t["cache_v"][:, bass.ds(h * P, P)]).then_inc(s_cache[s], 16)

            sp.wait_ge(s_smcopy, 7 * CHUNKS_M)
            head_weights(0, 0)
            sp.wait_ge(s_yu, START + CHUNKS_M)
            sp.wait_ge(s_backp, START + 8 * CHUNKS_M)
            sp.wait_ge(s_fin, CHUNKS_M)
            head_cache(0, 0)
            for qc in range(16):
                src = bass.AP(t["rpb"].tensor, qc, [[RPB_W, 8], [RPB_W * RPB_H, HEADS], [1, SPAN]])
                sp.dma_start(spans[qc * 8:(qc + 1) * 8, :, :], src).then_inc(s_span, 16)
            head_weights(1, 1)
            head_cache(1, 1)
            with sp.Fori(1, HEADS // 2) as i:
                for s in range(2):
                    h = 2 * i + s
                    sp.wait_ge(s_vmm, START + 2 * h - 2)
                    apart(sp)
                    head_weights(h, s)
                    sp.wait_ge(s_kcT, START + h - 1)
                    apart(sp)
                    sp.wait_ge(s_pv, START + 5 * h - 5)
                    apart(sp)
                    head_cache(h, s)
            sp.wait_ge(s_vmm, START + 2 * HEADS)
            sp.wait_ge(s_biasm, START + HEADS)
            sp.wait_ge(s_kn, START + HEADS)
            for s in range(2):
                sp.wait_ge(s_late_out[s], 16 + 16 * (4 * CHUNKS_M))
            for n in range(4):
                s = n % 2
                if n >= 2:
                    sp.wait_ge(s_omm, START + 5 * (n - 1))
                sp.dma_start(w_out_ring[s], w_out_v[:, :, n * BANK:(n + 1) * BANK]).then_inc(s_wout[s], 16)
                if n == 0:
                    sp.dma_start(x1, t["x"].rearrange("(t p) d -> p t d", p=P)).then_inc(s_xre, 16)
                if n >= 2:
                    sp.wait_ge(s_x1, START + 5 * (n - 1))
                for c in range(2):
                    sp.dma_start(gate1[s][:, c, :], mod_d[1 - c:2 - c, 2 * D + n * BANK:2 * D + (n + 1) * BANK]
                                 .to_broadcast([P, BANK])).then_inc(s_g1[s], 16)
            sp.wait_ge(s_pv, START + 5 * HEADS)
            sp.wait_ge(s_o, START + 5 * HEADS)
            for s in range(2):
                sp.wait_ge(s_kvout[s], 32 + 32 * (HEADS // 2))
            for dst, part in ((scale2, 4), (shift2, 3)):
                for c in range(2):
                    sp.dma_start(dst[:, c, :], mod_d[1 - c:2 - c, part * D:(part + 1) * D].to_broadcast([P, D]))\
                        .then_inc(s_n2load, 16)
            sp.dma_start(norm2, t["norm2"].to_broadcast([P, D])).then_inc(s_n2load, 16)
            sp.dma_start(w_r, t["w_router"].rearrange("(k p) e -> p k e", p=P)).then_inc(s_n2load, 16)
            def piece(e, j):
                if j < 4:
                    src = (w_gate_v, w_up_v)[j % 2][:, bass.ds(e, 1), :, (j // 2) * BANK:(j // 2 + 1) * BANK]
                    dst = w_ring[j % RING].rearrange("p (k n) -> p k n", k=KT)
                else:
                    src = w_down_v[:, bass.ds(e, 1), :, (j - 4) * 1024:(j - 3) * 1024]
                    dst = w_ring[j % RING].rearrange("p (k n) -> p k n", k=8)
                sp.dma_start(dst, src.rearrange("p e k n -> p (e k) n")).then_inc(s_w[j % RING], 16)

            def rest_of_expert(e):
                sp.wait_ge(s_dn, START + 4 * e)
                apart(sp)
                piece(e, 2)
                for j in range(3, 6):
                    sp.wait_ge(s_gu, START + 4 * e + j - 2)
                    apart(sp)
                    piece(e, j)

            sp.wait_ge(s_omm, START + 5 * 4)
            piece(0, 0)
            piece(0, 1)
            sp.wait_ge(s_x1, START + 5 * 4)
            sp.wait_ge(s_h2, TT)
            with sp.Fori(0, EXPERTS - 1) as e:
                rest_of_expert(e)
                for j in range(2):
                    if j == 0:
                        sp.wait_ge(s_gu, START + 4 * e + 4)
                    else:
                        sp.wait_ge(s_dn, START + 4 * e + 2)
                    apart(sp)
                    piece(e + 1, j)
            rest_of_expert(EXPERTS - 1)
            sp.wait_ge(s_scat, 16 * EXPERTS)

        @block.scalar
        def _(act):
            act.dma_start(x_in, t["x"][0:P, :]).then_inc(s_x, 16)
            act.dma_start(crow, t["c_rows"]).then_inc(s_small, 16)
            for name, r, n in (("b_glu", 0, 4), ("ssm_d", 4, 4), ("norm1", 8, 16), ("q_norm", 24, 1), ("k_norm", 25, 1)):
                act.dma_start(prow[r:r + n, :], t[name]).then_inc(s_small, 16)
            act.dma_start(ldt, t["log_dt"]).then_inc(s_rows, 16)
            for dst, name in ((r_are, "a_re"), (r_aim, "a_im"), (r_h0r, "h0_re"), (r_h0i, "h0_im")):
                act.dma_start(dst, t[name]).then_inc(s_rows, 16)
            act.wait_ge(s_bzero, 2)
            for c, name in enumerate(("b_re", "b_im")):
                v = bexp[:, c, :].rearrange("p (t g e) -> p t g e", t=32, g=2)
                for g in range(2):
                    src = t[name].rearrange("(r g) p c -> g p r c", g=2)[g]
                    act.dma_start(v[64 * g:64 * g + 64, :, g, :], src).then_inc(s_bload, 16)
            for c, name in enumerate(("c_re", "c_im")):
                v = cexp[:, c, :].rearrange("p (t l) -> p t l", t=8)
                for q in range(QS):
                    for g in range(2):
                        src = t[name].rearrange("(m q g) c p -> q g c m p", q=QS, g=2)[q, g]
                        row = 32 * q + 16 * g
                        act.dma_start(v[row:row + 16, :, 64 * g:64 * g + 64], src).then_inc(s_cload, 16)
            act.wait_ge(s_pt, 1)
            act.wait_ge(s_pcol, 1)
            act.activation(cT[:, :], bank(0, 32, 32), ACT.Silu).then_inc(s_ct, 1)
            act.wait_ge(s_rows, 80)
            act.activation(r_tmp[0][:, 0:2], ldt, ACT.Exp).then_inc(s_ract, 1)
            act.wait_ge(s_rdve, 1)
            act.activation(r_tmp[2], r_tmp[1], ACT.Exp).then_inc(s_ract, 1)
            act.wait_ge(s_rdve, 2)
            act.activation(r_tmp[6], r_tmp[4], ACT.Sin).then_inc(s_ract, 1)
            act.activation(r_tmp[7], r_tmp[5], ACT.Sin).then_inc(s_ract, 1)
            def x_sums(i):
                act.wait_ge(s_x, 16 * (i + 1))
                act.wait_ge(s_xt, START + 4 * i)
                act.activation(x_n, x_in, ACT.Square, accum_out=small[:, 0:1]).then_inc(s_xsum, 1)
                act.wait_ge(s_xsum, i + 1)
                act.wait_ge(s_eps, 1)
                act.activation(small[:, 1:2], small[:, 0:1], ACT.Sqrt, bias=eps[:, :], scale=1 / D).then_inc(s_xss, 1)

            def x_turned(i):
                for b in range(4):
                    act.wait_ge(s_xt, START + 4 * i + b + 1)
                    act.activation(hT[:, 4 * b:4 * b + 4, bass.ds(i * P, P)], bank(4 + b).rearrange("p (k t) -> p k t", k=4),
                                   ACT.Copy).then_inc(s_xev, 1)

            x_sums(0)
            x_turned(0)
            with act.Fori(0, ADA_MIX // 2) as i:
                act.wait_ge(s_xn, START + i + 1)
                act.dma_start(x_in, t["x"][bass.ds(i * P + P, P), :]).then_inc(s_x, 16)
                x_sums(i + 1)
                for s in range(2):
                    act.wait_ge(s_mod, START + 2 * i + s + 1)
                    act.dma_start(mod_d[:, bass.ds((2 * i + s) * BANK, BANK)], mod_ring[s]).then_inc(s_modout[s], 16)
                x_turned(i + 1)
            for n in range(4):
                act.wait_ge(s_bct, n + 1)
                c, d = n // 2, n % 2
                dst = BT.rearrange("p m (d c l) -> p d c m l", d=2, c=2)[:, d, c]
                act.activation(dst, bank(4 + n).rearrange("p (m l) -> p m l", m=4), ACT.Copy).then_inc(s_bcev, 1)
            for n in range(4):
                act.wait_ge(s_bct, 4 + n + 1)
                c, d = n // 2, n % 2
                src = bank(n).rearrange("p (m l) -> p m l", m=4)
                if c == 0:
                    act.activation(CT[:, :, d, 0, :], src, ACT.Copy)
                act.activation(CT[:, :, d, c + 1, :], src, ACT.Copy, scale=-1.0).then_inc(s_bcev, 1)
            act.wait_ge(s_bcev, 8)
            act.wait_ge(s_mods, 1)
            act.wait_ge(s_xev, START + 4 * TT)
            for k in range(KT):
                act.activation(hT[:, k, N_LAT:TOK], hT[:, k, N_LAT:TOK], ACT.Identity, bias=shift1[:, k:k + 1],
                               scale=scale1[:, k:k + 1]).then_inc(s_hctx, 1)

            def context_phases(m, j):
                act.wait_ge(s_table, 8 * m + j + 1)
                act.activation(rot[j % 3][:, :, N_LAT:TOK], rot[j % 3][:, :, 0:N_CTX], ACT.Copy).then_inc(s_rot, 1)

            act.wait_ge(s_tab, 1)
            with act.Fori(0, CHUNKS_M) as m:
                act.wait_ge(s_y, START + 8 * m)
                act.wait_ge(s_back, START + 8 * m)
                act.wait_ge(s_backp, START + 8 * m)
                act.wait_ge(s_finm, START + 8 * m)
                one = [(BTm.rearrange("p d c l -> p (d c l)"), BT[:, bass.ds(m, 1), :].rearrange("p m l -> p (m l)")),
                       (CTm.rearrange("p d c l -> p (d c l)"),
                        CT.rearrange("p m d c l -> p m (d c l)")[:, bass.ds(m, 1), :].rearrange("p m l -> p (m l)"))]
                for dst, src in ((E2m, E2), (E1m, E1)):
                    src = src.rearrange("p c (d m q) s -> p (c d) m (q s)", d=2, m=4)[:, :, bass.ds(m, 1), :]
                    one.append((dst.rearrange("p c d q s -> p (c d) (q s)"), src.rearrange("p a m n -> p a (m n)")))
                for n, which in enumerate((0, 5, 6)):
                    src = lanev[:, which, :].rearrange("p (d m q) -> p d m q", d=2, m=4)[:, :, bass.ds(m, 1), :]
                    one.append((lanem[:, n], src.rearrange("p d m q -> p d (m q)")))
                for dst, src in one:
                    act.activation(dst, src, ACT.Copy).then_inc(s_smcopy, 1)
                act.wait_ge(s_u, START + m + 1)
                act.wait_ge(s_yu, START + m)
                act.activation(uT[:, 0, 0:N_LAT].rearrange("p (r c) -> p r c", r=ROWS),
                               bank(6).rearrange("p (c r) -> p r c", r=ROWS), ACT.Copy).then_inc(s_uev, 1)
                act.activation(uT[:, 0, N_LAT:TOK], bank(7, N_CTX), ACT.Copy).then_inc(s_uev, 1)
                context_phases(m, 0)
                context_phases(m, 1)
                for j in range(8):
                    if j < 6:
                        context_phases(m, j + 2)
                    act.wait_ge(s_late_mm, START + 8 * m + j + 1)
                    act.wait_ge(s_late_out[j % 2], 16 + 16 * (4 * m + j // 2))
                    act.activation(row_late[j % 2], bank(6 + j % 2, ADA_LATE)[0:2, :], ACT.Copy).then_inc(s_late_row, 1)
                    act.wait_ge(s_late_row, START + 8 * m + j + 1)
                    act.dma_start(mod_d[:, bass.ds(m * (8 * ADA_LATE) + (2 * D + j * ADA_LATE), ADA_LATE)], row_late[j % 2])\
                        .then_inc(s_late_out[j % 2], 16)
                act.wait_ge(s_yu, START + m + 1)
                act.activation(gT[:, bass.ds(m, 1), :].rearrange("p m t -> p (m t)"), y_u, ACT.Gelu_apprx_tanh)\
                    .then_inc(s_g, 1)
            act.wait_ge(s_finT, 1)
            for c in range(2):
                act.activation(fin_rows[c], bank(6, P, P * c)[0:32, :], ACT.Copy).then_inc(s_sig, 1)
            act.wait_ge(s_sig, 2)
            act.dma_start(st_re, fin_rows[0]).then_inc(s_finout, 16)
            act.dma_start(st_im, fin_rows[1]).then_inc(s_finout, 16)
            for mo in range(4):
                act.wait_ge(s_glu, mo + 1)
                if mo >= 2:
                    act.wait_ge(s_mixu, mo - 1)
                act.activation(sig_u[mo % 2], bank(2 * (mo % 2), TOK), ACT.Sigmoid, bias=b_glu_c[:, mo:mo + 1])\
                    .then_inc(s_sig, 1)

            def slot(g, gs, k):
                if g is None:
                    return
                if k < 5:
                    n, b = 5 * g + k, (gs + k) % 2
                    act.wait_ge(s_mx, START + n + 1)
                    act.wait_ge(s_pT, START + n - 1)
                    w = 3 * P if k < 4 else P
                    act.activation(probs[b][:, 64:64 + w], bank(6, w), ACT.Exp, bias=small[:, 2 + b:3 + b],
                                   accum_out=small[:, 4 + b:5 + b]).then_inc(s_ex, 1)
                if 1 <= k < 6:
                    n = 5 * g + k - 1
                    act.wait_ge(s_pT, START + n + 1)
                    act.wait_ge(s_pv, START + n)
                    w = P * len(windows(k - 1))
                    if w == 4 * P:
                        act.activation(probsT_half[64:P, 0:P], bank(7, P)[64:P, :], ACT.Copy)
                        act.activation(probsT_half[0:64, P:2 * P], bank(7, P, 3 * P)[0:64, :], ACT.Copy)
                        act.activation(probsT[:, 0:2 * P], bank(7, 2 * P, P), ACT.Copy).then_inc(s_pTev, 1)
                    else:
                        act.activation(probsT[:, 0:w], bank(7, w), ACT.Copy).then_inc(s_pTev, 1)

            def root(h, which):
                act.wait_ge(s_ss, START + 2 * h + which + 1)
                act.activation(rstd, bank(4, TOK), ACT.Sqrt, bias=eps[:, :], scale=1 / HD).then_inc(s_root, 1)

            def step(h, s, pair, g):
                gs = 1 - s
                if h is None:
                    for k in range(7):
                        slot(g, gs, k)
                    return
                slot(g, gs, 0)
                slot(g, gs, 1)
                act.wait_ge(s_qmm, h + 1)
                act.wait_ge(s_ss, START + 2 * h)
                act.activation(sq[0], bank(2 * s, TOK), ACT.Square).then_inc(s_sq, 1)
                act.wait_ge(s_kcT, START + h + 1)
                act.activation(kcT[s], bank(5, P), ACT.Copy).then_inc(s_kcev, 1)
                act.wait_ge(s_kn, START + h)
                root(h, 0)
                slot(g, gs, 2)
                slot(g, gs, 3)
                act.wait_ge(s_kmm, h + 1)
                act.activation(sq[1], bank(2 - 2 * s, TOK), ACT.Square).then_inc(s_sq, 1)
                slot(g, gs, 4)
                act.wait_ge(s_qn, h + 1)
                root(h, 1)
                slot(g, gs, 5)
                act.wait_ge(s_vmm, START + 2 * h + 1)
                act.wait_ge(s_pv, START + 5 * h - 5)
                act.activation(vS[s][:, 0:4, :].rearrange("p t n -> p (t n)"), bank(2 * s), ACT.Copy).then_inc(s_vev, 1)
                act.wait_ge(s_kvout[s], 32 + 32 * pair)
                act.wait_ge(s_knT, h + 1)
                act.activation(knat[s], bank(5, P), ACT.Copy).then_inc(s_knev, 1)
                act.wait_ge(s_knev, START + h + 1)
                act.dma_start(new_k[:, bass.ds(h * P, P)], knat[s]).then_inc(s_kvout[s], 16)
                act.wait_ge(s_vmm, START + 2 * h + 2)
                act.activation(vS[s][:, 4, :], bank(2 * s + 1, P), ACT.Copy).then_inc(s_vev, 1)
                act.wait_ge(s_vev, START + 2 * h + 2)
                act.dma_start(new_v[:, bass.ds(h * P, P)], vS[s][:, 4, :]).then_inc(s_kvout[s], 16)
                slot(g, gs, 6)

            act.wait_ge(s_padz, 1)
            heads_in_turn(act, step)

            with act.Fori(0, 2) as i:
                for s in range(2):
                    n = 2 * i + s
                    for tt in range(TT):
                        act.wait_ge(s_x1, START + 5 * n + tt + 1)
                        act.wait_ge(s_ss2, START + 5 * n + tt)
                        act.activation(junk, x1[:, tt, bass.ds(n * BANK, BANK)], ACT.Square,
                                       accum_out=ssq[:, tt, bass.ds(n, 1)]).then_inc(s_ss2, 1)

            for tt in range(TT):
                act.wait_ge(s_ssum, tt + 1)
                act.activation(stat[:, tt, 5:6], stat[:, tt, 0:1], ACT.Sqrt, bias=eps[:, :], scale=1 / D).then_inc(s_nroot, 1)
            for tt in range(TT):
                act.wait_ge(s_h2, tt + 1)
                act.dma_start(y_out[tt * P:(tt + 1) * P, :], x1[:, tt, :]).then_inc(s_x1out, 16)
                act.dma_start(h2_d[tt * P:(tt + 1) * P, :], h2[tt % 2]).then_inc(s_h2out[tt % 2], 16)
                for b in range(4):
                    act.wait_ge(s_h2T, 4 * tt + b + 1)
                    if tt >= 2:
                        act.wait_ge(s_logit, tt - 1)
                    act.activation(h2T[tt % 2][:, 4 * b:4 * b + 4, :], bank(b).rearrange("p (k t) -> p k t", k=4), ACT.Copy)\
                        .then_inc(s_h2Tev, 1)
                act.wait_ge(s_nmx, tt + 1)
                act.activation(aff[:, tt, :], bank(4 + tt % 2, 16), ACT.Exp, bias=stat[:, tt, 2:3],
                               accum_out=stat[:, tt, 3:4]).then_inc(s_eaff, 1)
            act.wait_ge(s_h2out[0], 48)
            act.wait_ge(s_h2out[1], 32)
            act.wait_ge(s_logit, TT)
            act.dma_start(gate2[0:CAP_L, :], mod_d[1:2, 5 * D:6 * D].to_broadcast([CAP_L, D])).then_inc(s_gate2, 16)
            act.dma_start(gate2[CAP_L:SLOTS, :], mod_d[0:1, 5 * D:6 * D].to_broadcast([CAP_C, D])).then_inc(s_gate2, 16)

            def tokens_out(e, s):
                for b in range(4):
                    act.wait_ge(s_xsT, 4 * e + b + 1)
                    act.activation(xsT[s][:, 4 * b:4 * b + 4, :].rearrange("p k s -> p (k s)"),
                                   bank(5 - b % 2, 4 * SLOTS), ACT.Copy).then_inc(s_xsev, 1)

            def hidden_out(e, f):
                act.wait_ge(s_hhT, START + 2 * e + f + 1)
                act.activation(actT[:, 4 * f:4 * f + 4, :].rearrange("p k s -> p (k s)"), bank(4 + f, 4 * SLOTS), ACT.Copy)\
                    .then_inc(s_hhev, 1)

            def expert(e, s, last=False):
                for f in range(2):
                    act.wait_ge(s_gu, START + 4 * e + 2 * f + 1)
                    act.wait_ge(s_hh, START + 2 * e)
                    act.activation(act_g[:, f * BANK:(f + 1) * BANK], bank(2 * f)[0:SLOTS, :], ACT.Silu).then_inc(s_sg, 1)
                act.wait_ge(s_dn, START + 4 * e)
                hidden_out(e, 0)
                if not last:
                    tokens_out(e + 1, 1 - s)
                hidden_out(e, 1)

            act.wait_ge(s_x1out, 16 * TT)
            tokens_out(0, 0)
            with act.Fori(0, EXPERTS // 2 - 1) as i:
                expert(2 * i, 0)
                expert(2 * i + 1, 1)
            expert(EXPERTS - 2, 0)
            expert(EXPERTS - 1, 1, last=True)

        @block.tensor
        def _(pe):
            def turn(dst, src, parts=P):
                return pe.transpose(dst, src, ident[0:parts, 0:parts])

            pe.wait_ge(s_const, 16)
            pe.wait_ge(s_small, 96)
            turn(bank(0, 26), prow, 26)
            turn(bank(0, 32, 32), crow, 32).then_inc(s_pt, 1)
            pe.wait_ge(s_rows, 80)
            pe.wait_ge(s_rdve, 3)
            for n, src in enumerate((r_tmp[2], r_tmp[7], r_tmp[6], r_tmp[10], r_tmp[11], r_h0r, r_h0i)):
                last = turn(bank(1, 32, 32 * n), src, 32)
            last.then_inc(s_lane, 1)
            def turn_x(i):
                pe.wait_ge(s_xn, START + i + 1)
                pe.wait_ge(s_xev, START + 4 * i)
                for b in range(4):
                    for k in range(4):
                        last = turn(bank(4 + b, P, k * P), x_n[:, (4 * b + k) * P:(4 * b + k + 1) * P])
                    last.then_inc(s_xt, 1)

            turn_x(0)
            pe.wait_ge(s_ct, 1)
            with pe.Fori(0, ADA_MIX // 2) as i:
                for s in range(2):
                    pe.wait_ge(s_ada[s], 32 * (i + 1))
                    pe.wait_ge(s_mod, START + 2 * i + s - 1)
                    for k in range(KT):
                        last = pe.matmul(bank(2 + s)[0:2, :], cTv[:, :, k], w_ada_ring[s][:, k, :],
                                         start=(k == 0), stop=(k == KT - 1))
                    last.then_inc(s_ada_mm, 1)
                turn_x(i + 1)
            pe.wait_ge(s_bbar, 1)
            pe.wait_ge(s_xev, START + 4 * TT)
            for n in range(4):
                c, d = n // 2, n % 2
                for m in range(4):
                    last = turn(bank(4 + n, P, m * P), bbar[:, c, (d * 4 + m) * P:(d * 4 + m + 1) * P])
                last.then_inc(s_bct, 1)
            pe.wait_ge(s_cload, 256)
            pe.wait_ge(s_mod, START + ADA_MIX)
            pe.wait_ge(s_pcol, 2)
            for n in range(4):
                c, d = n // 2, n % 2
                for m in range(4):
                    last = turn(bank(n, P, m * P), cexp[:, c, (d * 4 + m) * P:(d * 4 + m + 1) * P])
                last.then_inc(s_bct, 1)
            pe.wait_ge(s_modrow, 32)
            pe.wait_ge(s_bcev, 4)
            turn(bank(4, 64), modrow, 64).then_inc(s_modT, 1)

            def bu(m, j):
                q, d = j // 2, j % 2
                pe.wait_ge(s_rmul, START + 8 * m + j)
                rows = slice(32 * q, 32 * q + 32)
                for c in range(2):
                    for col, n in ((0, N_LAT), (N_LAT, N_CTX)):
                        last = pe.matmul(bank(2 * c, n, col), BTm[rows, d, c, :], uT[rows, d, col:col + n],
                                         start=True, stop=True)
                last.then_inc(s_bu, 1)

            def y(m, j):
                q, d = j // 2, j % 2
                pe.wait_ge(s_back, START + 8 * m + j + 1)
                pe.wait_ge(s_backp, START + 8 * m + j + 1)
                if j == 0:
                    pe.wait_ge(s_yu, START + m)
                for col, n in ((0, N_LAT), (N_LAT, N_CTX)):
                    for x, kind in enumerate((0, 1, 2, 2)):
                        last = pe.matmul(bank(4, n, col)[32 * q:32 * q + 32, :], CTm[:, d, kind, 32 * q:32 * q + 32],
                                         back[:, x, col:col + n], start=(d == 0 and x == 0), stop=(d == 1 and x == 3))
                last.then_inc(s_y, 1)

            def late_rows(m, j):
                pe.wait_ge(s_late[j % 2], 32 * (4 * m + j // 2 + 1))
                pe.wait_ge(s_late_row, START + 8 * m + j - 1)
                dst = bank(6 + j % 2, ADA_LATE)[0:2, :]
                for k in range(KT):
                    pe.matmul(dst, cTv[:, :, k], w_late[j % 2][:, k, :], start=(k == 0), stop=False)
                pe.matmul(dst, ones[0:1, 0:2], b_late[j % 2], start=False, stop=True).then_inc(s_late_mm, 1)

            with pe.Fori(0, CHUNKS_M) as m:
                pe.wait_ge(s_wu, 16 * (m + 1))
                pe.wait_ge(s_uev, START + 2 * m)
                pe.wait_ge(s_late_row, START + 8 * m)
                pe.wait_ge(s_bcev, 8)
                for col, n, ready in ((0, N_LAT, s_hlat), (N_LAT, N_CTX, s_hctx)):
                    for k in range(KT):
                        pe.wait_ge(ready, k + 1)
                        last = pe.matmul(bank(6, n, col), w_u[:, k, :], hT[:, k, col:col + n], start=(k == 0),
                                         stop=(k == KT - 1))
                last.then_inc(s_u, 1)
                pe.wait_ge(s_smcopy, 7 * (m + 1))
                pe.wait_ge(s_uev, START + 2 * (m + 1))
                pe.wait_ge(s_urev, m + 1)
                bu(m, 0)
                for j in range(8):
                    if j < 7:
                        bu(m, j + 1)
                    late_rows(m, j)
                    y(m, j)
            pe.wait_ge(s_fin, CHUNKS_M)
            pe.wait_ge(s_late_row, START + 8 * CHUNKS_M)
            for c in range(2):
                last = turn(bank(6, P, P * c)[0:32, :], fin[:, 32 * c:32 * c + 32])
            last.then_inc(s_finT, 1)
            pe.wait_ge(s_wglu, 16)
            pe.wait_ge(s_g, START + CHUNKS_M)
            for mo in range(4):
                if mo >= 2:
                    pe.wait_ge(s_sig, 2 + mo - 1)
                for col, n in ((0, N_LAT), (N_LAT, N_CTX)):
                    for mk in range(4):
                        last = pe.matmul(bank(2 * (mo % 2), n, col), w_glu[:, mk, mo * P:(mo + 1) * P],
                                         gT[:, mk, col:col + n], start=(mk == 0), stop=(mk == 3))
                last.then_inc(s_glu, 1)

            def slot(g, gs, k):
                if g is None:
                    return
                if k < 5:
                    n = 5 * g + k
                    pe.wait_ge(s_ex, START + n)
                    if k == 0:
                        pe.wait_ge(s_kn, START + g + 1)
                        pe.wait_ge(s_kcev, START + g + 1)
                        pe.wait_ge(s_vev, START + 2 * g + 2)
                    q = qT[gs][:, k * P:(k + 1) * P]
                    if k < 4:
                        pe.matmul(bank(6, 256), q, kT[gs][:, KEY_START[k]:KEY_START[k] + 256], start=True, stop=True)
                        pe.matmul(bank(6, P, 256), q, kcT[gs], start=True, stop=True).then_inc(s_sc, 1)
                    else:
                        pe.matmul(bank(6, P), q, kT[gs][:, N_LAT:TOK], start=True, stop=True).then_inc(s_sc, 1)
                if 1 <= k < 6:
                    n = 5 * g + k - 1
                    pe.wait_ge(s_pn, n + 1)
                    pe.wait_ge(s_pTev, START + n)
                    for x, (col, _, _, _) in enumerate(windows(k - 1)):
                        last = turn(bank(7, P, x * P), probs[(gs + k - 1) % 2][:, col:col + P])
                    last.then_inc(s_pT, 1)
                if 2 <= k:
                    a, n = k - 2, 5 * g + k - 2
                    pe.wait_ge(s_pTev, START + n + 1)
                    pe.wait_ge(s_o, START + n)
                    if a == 0 and more_heads(g):
                        pe.wait_ge(s_root, START + 2 * g + 3)
                    if a == 3 and more_heads(g):
                        pe.wait_ge(s_root, START + 2 * g + 4)
                    if a == 4 and more_heads(g):
                        pe.wait_ge(s_knev, START + g + 2)
                    dst = bank(5, P)
                    ws = windows(a)
                    for x, (_, tile, lo, hi) in enumerate(ws):
                        v = vc[gs] if tile is None else vS[gs][:, tile, :]
                        if len(ws) < 4:
                            p = probsT[:, x * P:(x + 1) * P]
                        else:
                            p = {0: probsT_half[:, 0:P], 1: probsT[:, 0:P], 2: probsT[:, P:2 * P],
                                 3: probsT_half[:, P:2 * P]}[x]
                        last = pe.matmul(dst, v, p, start=(x == 0),
                                         stop=(x == len(ws) - 1))
                    last.then_inc(s_pv, 1)

            def values(h, s, tile):
                if tile == 0:
                    pe.wait_ge(s_qn, h + 1)
                for k in range(KT):
                    last = pe.matmul(bank(2 * s, P, tile * P), hT[:, k, tile * P:(tile + 1) * P], w_qkv[s][:, k, 2, :],
                                     start=(k == 0), stop=(k == KT - 1))
                if tile >= 3:
                    last.then_inc(s_vmm, 1)

            def step(h, s, pair, g):
                gs = 1 - s
                if h is None:
                    for k in range(7):
                        slot(g, gs, k)
                    return
                pe.wait_ge(s_wqkv[s], 48 * (pair + 1))
                pe.wait_ge(s_kn, START + h)

                def part(which, dst, col, n, ks):
                    for k in ks:
                        last = pe.matmul(bank(dst, n, col), w_qkv[s][:, k, which, :], hT[:, k, col:col + n],
                                         start=(k == 0), stop=(k == KT - 1))
                    return last

                part(0, 2 * s, 0, N_LAT, range(0, KT // 2))
                slot(g, gs, 0)
                part(0, 2 * s, 0, N_LAT, range(KT // 2, KT))
                slot(g, gs, 1)
                part(0, 2 * s, N_LAT, N_CTX, range(KT)).then_inc(s_qmm, 1)
                pe.wait_ge(s_vev, START + 2 * h)
                part(1, 2 - 2 * s, 0, N_LAT, range(0, KT // 4))
                pe.wait_ge(s_cache[s], 32 * (pair + 1))
                pe.wait_ge(s_knev, START + h)
                pe.wait_ge(s_o, START + 5 * h - 5)
                turn(bank(5, P), kc_in[s]).then_inc(s_kcT, 1)
                part(1, 2 - 2 * s, 0, N_LAT, range(KT // 4, KT // 2))
                pe.wait_ge(s_sq, START + 2 * h + 1)
                pe.wait_ge(s_kcev, START + h + 1)
                for col, n in ((0, N_LAT), (N_LAT, N_CTX)):
                    last = pe.matmul(bank(4, n, col), ones, sq[0][:, col:col + n], start=True, stop=True)
                last.then_inc(s_ss, 1)
                slot(g, gs, 2)
                part(1, 2 - 2 * s, 0, N_LAT, range(KT // 2, KT))
                slot(g, gs, 3)
                part(1, 2 - 2 * s, N_LAT, N_CTX, range(KT)).then_inc(s_kmm, 1)
                values(h, s, 0)
                slot(g, gs, 4)
                values(h, s, 1)
                pe.wait_ge(s_sq, START + 2 * h + 2)
                pe.wait_ge(s_o, START + 5 * h - 2)
                for col, n in ((0, N_LAT), (N_LAT, N_CTX)):
                    last = pe.matmul(bank(4, n, col), ones, sq[1][:, col:col + n], start=True, stop=True)
                last.then_inc(s_ss, 1)
                values(h, s, 2)
                slot(g, gs, 5)
                values(h, s, 3)
                pe.wait_ge(s_kn, START + h + 1)
                pe.wait_ge(s_o, START + 5 * h - 1)
                turn(bank(5, P), kT[s][:, N_LAT:TOK]).then_inc(s_knT, 1)
                values(h, s, 4)
                slot(g, gs, 6)

            pe.wait_ge(s_sig, 2 + 4)
            heads_in_turn(pe, step)

            pe.wait_ge(s_mixu, 4)
            pe.wait_ge(s_o, START + 5 * HEADS)
            with pe.Fori(0, 2) as i:
                for s in range(2):
                    pe.wait_ge(s_wout[s], 16 * (i + 1))
                    for tt in range(TT):
                        pe.wait_ge(s_x1, START + 10 * i + 5 * s + tt - 4)
                        for k in range(MIX_T):
                            last = pe.matmul(bank(tt), mixT[:, k, tt * P:(tt + 1) * P], w_out_ring[s][:, k, :],
                                             start=(k == 0), stop=(k == MIX_T - 1))
                        last.then_inc(s_omm, 1)

            pe.wait_ge(s_x1, START + 5 * 4)
            pe.wait_ge(s_n2load, 96)
            for tt in range(TT):
                pe.wait_ge(s_h2, tt + 1)
                for b in range(4):
                    if tt:
                        pe.wait_ge(s_h2Tev, 4 * (tt - 1) + b + 1)
                    for k in range(4):
                        last = turn(bank(b, P, k * P), h2[tt % 2][:, (4 * b + k) * P:(4 * b + k + 1) * P])
                    last.then_inc(s_h2T, 1)
                if tt >= 2:
                    pe.wait_ge(s_aff, tt - 1)
                for b in range(4):
                    pe.wait_ge(s_h2Tev, 4 * tt + b + 1)
                    for k in range(4 * b, 4 * b + 4):
                        last = pe.matmul(bank(4 + tt % 2, 16), h2T[tt % 2][:, k, :], w_r[:, k, :], start=(k == 0),
                                         stop=(k == KT - 1))
                last.then_inc(s_logit, 1)
            for tt in range(TT):
                pe.wait_ge(s_aff, tt + 1)
                dst = bank(6, P, P * tt) if tt < 4 else bank(7, P)
                last = turn(dst[0:EXPERTS, :], aff[:, tt, :])
            last.then_inc(s_affT, 1)
            pe.wait_ge(s_top, 1)
            turn(bank(0, 16)[0:SLOTS, :], top_v, 16)
            turn(bank(0, 16, 16)[0:SLOTS, :], top_f, 16).then_inc(s_topT, 1)

            def turn_tokens(e, s, landed, first=False):
                pe.wait_ge(s_gath[s], landed)
                for b in range(4):
                    if b == 1 and not first:
                        pe.wait_ge(s_hhev, 2 * e - 1)
                    if b >= 2:
                        pe.wait_ge(s_xsev, 4 * e + b - 1)
                    for k in range(4):
                        last = turn(bank(5 - b % 2, SLOTS, k * SLOTS), xs[s][:, (4 * b + k) * P:(4 * b + k + 1) * P], SLOTS)
                    last.then_inc(s_xsT, 1)

            def turn_hidden(e, f):
                pe.wait_ge(s_hh, START + 2 * e + f + 1)
                for k in range(4):
                    last = turn(bank(4 + f, SLOTS, k * SLOTS), act_h[:, (4 * f + k) * P:(4 * f + k + 1) * P], SLOTS)
                last.then_inc(s_hhT, 1)

            def expert(e, s, pair, last_one=False):
                pe.wait_ge(s_xsev, 4 * e + 4)
                for j in range(4):
                    pe.wait_ge(s_w[j % RING], 16 * (2 * e + j // RING + 1))
                    pe.wait_ge(s_hh, START + 2 * e)
                    w = w_ring[j % RING].rearrange("p (k n) -> p k n", k=KT)
                    for k in range(KT):
                        last = pe.matmul(bank(j)[0:SLOTS, :], xsT[s][:, k, :], w[:, k, :], start=(k == 0),
                                         stop=(k == KT - 1))
                    last.then_inc(s_gu, 1)
                turn_hidden(e, 0)
                if not last_one:
                    turn_tokens(e + 1, 1 - s, 16 * (pair + 1 + s))
                    pe.wait_ge(s_xsev, 4 * e + 7)
                turn_hidden(e, 1)
                pe.wait_ge(s_hhev, 2 * e + 2)
                for j in range(2):
                    pe.wait_ge(s_w[(4 + j) % RING], 16 * (2 * e + 2))
                    w = w_ring[(4 + j) % RING].rearrange("p (k n) -> p k n", k=8)
                    for c in range(2):
                        pe.wait_ge(s_ye, START + 4 * e + 2 * j + c - 1)
                        for k in range(8):
                            last = pe.matmul(bank(6 + c)[0:SLOTS, :], actT[:, k, :], w[:, k, c * BANK:(c + 1) * BANK],
                                             start=(k == 0), stop=(k == 7))
                        last.then_inc(s_dn, 1)

            turn_tokens(0, 0, 16, first=True)
            with pe.Fori(0, EXPERTS // 2 - 1) as i:
                expert(2 * i, 0, i)
                expert(2 * i + 1, 1, i)
            expert(EXPERTS - 2, 0, EXPERTS // 2 - 1)
            expert(EXPERTS - 1, 1, EXPERTS // 2 - 1, last_one=True)

        @block.vector
        def _(dve):
            ch = Chain(dve, s_dve)
            TT_, TS_, STT = dve.tensor_tensor, dve.tensor_scalar, dve.scalar_tensor_tensor
            dve.wait_ge(s_pt, 1)
            dve.tensor_copy(pcol[:, :], bank(0, 26)).then_inc(s_pcol, 1)
            dve.wait_ge(s_pcol, 1)
            ch.link(TS_(q_gain[:, :], q_gain_raw, HD ** -0.5, None, ALU.mult))
            dve.memset(eps[:, :], EPS).then_inc(s_eps, 1)
            dve.wait_ge(s_rows, 80)
            dve.wait_ge(s_ract, 1)
            r = r_tmp
            for half in range(2):
                cols = slice(64 * half, 64 * half + 64)
                dt = r[0][:, half:half + 1]
                ch.mark(TS_(r[3][:, cols], r_aim[:, cols], dt, None, ALU.mult))
                last = TS_(r[1][:, cols], r_are[:, cols], dt, None, ALU.mult)
                if half == 0:
                    ch.mark(last)
            last.then_inc(s_rdve, 1)
            ch.wait()
            MAGIC = 1.5 * 2.0 ** 23
            C1 = 6.28125
            C2 = float(np.float32(np.floor((2 * math.pi - C1) * 2 ** 21) / 2 ** 21))
            C3 = 2 * math.pi - C1 - C2
            ch.link(TS_(r[5], r[3], 1 / (2 * math.pi), MAGIC, ALU.mult, ALU.add))
            ch.link(TS_(r[5], r[5], MAGIC, None, ALU.subtract))
            ch.link(STT(r[4], r[5], -C1, r[3], ALU.mult, ALU.add))
            ch.link(STT(r[4], r[5], -C2, r[4], ALU.mult, ALU.add))
            ch.link(STT(r[4], r[5], -C3, r[4], ALU.mult, ALU.add))
            ch.link(TS_(r[4], r[4], 3.1415925, -3.1415925, ALU.min, ALU.max))
            ch.link(STT(r[5], r[4], -1.0, r[4], ALU.mult, ALU.max))
            TS_(r[5], r[5], -1.0, math.pi / 2, ALU.mult, ALU.add).then_inc(s_rdve, 1)
            dve.wait_ge(s_ract, 4)
            dve.wait_ge(s_rdve, 2)
            ch.mark(TT_(r[8], r[2], r[7], ALU.mult))
            ch.mark(TT_(r[9], r[2], r[6], ALU.mult))
            ch.mark(TT_(r[12], r_are, r_are, ALU.mult))
            ch.link(TT_(r[13], r_aim, r_aim, ALU.mult))
            ch.mark(TS_(r[8], r[8], 1.0, None, ALU.subtract))
            ch.link(TT_(r[12], r[12], r[13], ALU.add))
            ch.mark(dve.reciprocal(r[12], r[12]))
            ch.mark(TT_(r[10], r[8], r_are, ALU.mult))
            ch.mark(TT_(r[13], r[9], r_aim, ALU.mult))
            ch.mark(TT_(r[11], r[9], r_are, ALU.mult))
            ch.link(TT_(r[8], r[8], r_aim, ALU.mult))
            ch.mark(TT_(r[10], r[10], r[13], ALU.add))
            ch.link(TT_(r[11], r[11], r[8], ALU.subtract))
            ch.mark(TT_(r[10], r[10], r[12], ALU.mult))
            TT_(r[11], r[11], r[12], ALU.mult).then_inc(s_rdve, 1)
            dve.wait_ge(s_lane, 1)
            dve.tensor_copy(lane[:, :], bank(1, 224)).then_inc(s_pcol, 1)
            def x_norm(i):
                dve.wait_ge(s_xss, i + 1)
                ch.link(dve.reciprocal(small[:, 9:10], small[:, 1:2]))
                TS_(x_n, x_in, small[:, 9:10], None, ALU.mult).then_inc(s_xn, 1)

            x_norm(0)
            with dve.Fori(0, ADA_MIX // 2) as i, ch.body(i, 1):
                x_norm(i + 1)
                for s in range(2):
                    dve.wait_ge(s_ada_mm, START + 2 * i + s + 1)
                    dve.wait_ge(s_modout[s], 16 + 16 * i)
                    TT_(mod_ring[s], bank(2 + s)[0:2, :], b_ada_ring[s], ALU.add).then_inc(s_mod, 1)
            ch.passed(ADA_MIX // 2)
            dve.wait_ge(s_modT, 1)
            for c in range(2):
                ch.mark(STT(scale1[:, c * 16:c * 16 + 16], bank(4, 16, c * 32 + 16), 1.0, norm1_c, ALU.add, ALU.mult))
                last = dve.tensor_copy(shift1[:, c * 16:c * 16 + 16], bank(4, 16, c * 32))
                if c == 0:
                    ch.mark(last)
            last.then_inc(s_mods, 1)
            ch.wait()
            dve.wait_ge(s_mods, 1)
            dve.wait_ge(s_xev, START + 4 * TT)
            for k in range(KT):
                TS_(hT[:, k, 0:N_LAT], hT[:, k, 0:N_LAT], scale1[:, 16 + k:17 + k], shift1[:, 16 + k:17 + k], ALU.mult,
                    ALU.add).then_inc(s_hlat, 1)

            def rotate_in(m, j):
                dve.wait_ge(s_rot, 8 * m + j + 1)
                dve.wait_ge(s_bu, 8 * m + j + 1)
                R = rot[j % 3]
                for x, (src, ph) in enumerate(((0, 0), (2, 1), (2, 0), (0, 1))):
                    last = TT_(prod[j % 2][:, x], bank(src, TOK), R[:, ph], ALU.mult)
                last.then_inc(s_rmul, 1)

            def scan(m, j):
                q, d = j // 2, j % 2
                n = 8 * m + j
                dve.wait_ge(s_radd, n + 1)
                dve.wait_ge(s_backp, START + n)
                mag = lanem[:, 0, d, q:q + 1]
                for c in range(2):
                    dve.tensor_tensor_scan(gsc[:, c, 0:N_LAT], mag.to_broadcast([P, N_LAT]), rin[:, c, 0:N_LAT],
                                           lanem[:, 1 + c, d, q:q + 1], ALU.mult, ALU.add)
                    last = dve.tensor_tensor_scan(gsc[:, c, N_LAT:TOK], mag.to_broadcast([P, N_CTX]),
                                                  rin[:, c, N_LAT:TOK], 0.0, ALU.mult, ALU.add)
                    if c == 0:
                        ch.mark(last)
                last.then_inc(s_scan, 1)

            def rotate_back(m, j):
                q, d = j // 2, j % 2
                n = 8 * m + j
                dve.wait_ge(s_scan, START + n + 1)
                ch.wait()
                dve.wait_ge(s_y, START + n)
                for x, (c, ph) in enumerate(((0, 0), (1, 1))):
                    for sl in ((slice(0, TOK),) if d == 0 else (slice(0, N_LAT), slice(N_LAT, TOK))):
                        dst = back[:, x, sl] if d == 0 else back[:, x, sl][:, ::-1]
                        last = TT_(dst, gsc[:, c, sl], rot[j % 3][:, ph, sl], ALU.mult)
                last.then_inc(s_back, 1)
                dve.wait_ge(s_back, START + n + 1)
                dve.wait_ge(s_backp, START + n + 1)
                at_ = TOK - 1 if d == 0 else N_LAT
                ch.mark(TT_(finm[:, 0, d, q:q + 1], back[:, 0, at_:at_ + 1], back[:, 1, at_:at_ + 1], ALU.subtract))
                TT_(finm[:, 1, d, q:q + 1], back[:, 2, at_:at_ + 1], back[:, 3, at_:at_ + 1], ALU.add).then_inc(s_finm, 1)

            with dve.Fori(0, CHUNKS_M) as m, ch.body(m, 18):
                dve.wait_ge(s_smcopy, 7 * (m + 1))
                dve.wait_ge(s_uev, START + 2 * (m + 1))
                ch.mark(dve.tensor_copy(uT[:, 1, 0:N_LAT][:, ::-1], uT[:, 0, 0:N_LAT]))
                dve.tensor_copy(uT[:, 1, N_LAT:TOK][:, ::-1], uT[:, 0, N_LAT:TOK]).then_inc(s_urev, 1)
                rotate_in(m, 0)
                for j in range(8):
                    if j < 7:
                        rotate_in(m, j + 1)
                    scan(m, j)
                    rotate_back(m, j)
                dve.wait_ge(s_finm, START + 8 * (m + 1))
                ch.mark(dve.tensor_copy(
                    fin[:, :].rearrange("p (a m q) -> p a m q", a=4, m=4)[:, :, bass.ds(m, 1), :].rearrange("p a m q -> p a (m q)"),
                    finm.rearrange("p c d q -> p (c d) q")))
                dve.wait_ge(s_y, START + 8 * (m + 1))
                dve.wait_ge(s_g, START + m)
                STT(y_u, uT[:, 0, :], ssm_d_c[:, bass.ds(m, 1)], bank(4, TOK), ALU.mult, ALU.add).then_inc(s_yu, 1)
            ch.passed(18 * CHUNKS_M)
            ch.link(dve.tensor_copy(small[:, 8:9], fin[:, 0:1]))
            dve.sem_inc(s_fin, CHUNKS_M)
            for mo in range(4):
                dve.wait_ge(s_sig, 2 + mo + 1)
                dve.wait_ge(s_g, START + CHUNKS_M)
                ch.mark(TT_(mixT[:, HEADS + mo, 0:N_LAT].rearrange("p (c r) -> p r c", r=ROWS),
                            gT[:, mo, 0:N_LAT].rearrange("p (r c) -> p r c", r=ROWS),
                            sig_u[mo % 2][:, 0:N_LAT].rearrange("p (r c) -> p r c", r=ROWS), ALU.mult))
                TT_(mixT[:, HEADS + mo, N_LAT:TOK], gT[:, mo, N_LAT:TOK], sig_u[mo % 2][:, N_LAT:TOK], ALU.mult)\
                    .then_inc(s_mixu, 1)

            dve.wait_ge(s_finout, 32)
            for b in range(2):
                ch.link(dve.memset(probs[b][:, 0:64], 0.0))
            dve.memset(probsT_half, 0.0).then_inc(s_padz, 1)

            def slot(g, gs, k):
                if g is None:
                    return
                if k < 5:
                    n, b = 5 * g + k, (gs + k) % 2
                    dve.wait_ge(s_sc, n + 1)
                    w = 3 * P if k < 4 else P
                    if k < 4:
                        dve.wait_ge(s_biasm, START + g + 1)
                        TT_(bank(6, 256), bank(6, 256), biasm[gs][:, VARIANT[k], :], ALU.add).then_inc(s_biased, 1)
                        dve.wait_ge(s_biased, 4 * g + k + 1)
                    dve.tensor_reduce(small[:, 2 + b:3 + b], bank(6, w), AX, ALU.max, negate=True).then_inc(s_mx, 1)
                if k >= 2:
                    a, n = k - 2, 5 * g + k - 2
                    dve.wait_ge(s_pv, START + n + 1)
                    dve.tensor_copy(mixT[:, bass.ds(g, 1), a * P:(a + 1) * P].rearrange("p g t -> p (g t)"),
                                    bank(5, P)).then_inc(s_o, 1)
                if k < 5:
                    dve.wait_ge(s_ex, START + 5 * g + k + 1)
                    dve.reciprocal(small[:, 6 + b:7 + b], small[:, 4 + b:5 + b]).then_inc(s_rsum, 1)
                    dve.wait_ge(s_rsum, 5 * g + k + 1)
                    TS_(probs[b][:, 64:64 + w], probs[b][:, 64:64 + w], small[:, 6 + b:7 + b], None, ALU.mult)\
                        .then_inc(s_pn, 1)

            def normed(h, s, which, dst, src, gain, done):
                dve.wait_ge(s_root, START + 2 * h + which + 1)
                dve.reciprocal(rstd, rstd).then_inc(s_rstd, 1)
                dve.wait_ge(s_rstd, 2 * h + which + 1)
                STT(dst, bank(src, TOK), gain, rstd, ALU.mult, ALU.mult).then_inc(done, 1)

            def step(h, s, pair, g):
                gs = 1 - s
                if h is None:
                    for k in range(7):
                        slot(g, gs, k)
                    return
                slot(g, gs, 0)
                slot(g, gs, 1)
                normed(h, s, 0, qT[s], 2 * s, q_gain[:, :], s_qn)
                for k in range(2, 5):
                    slot(g, gs, k)
                normed(h, s, 1, kT[s], 2 - 2 * s, k_gain, s_kn)
                slot(g, gs, 5)
                slot(g, gs, 6)

            heads_in_turn(dve, step)

            dve.wait_ge(s_xre, 16)
            with dve.Fori(0, 2) as i, ch.body(i, 10):
                for s in range(2):
                    n = 2 * i + s
                    dve.wait_ge(s_g1[s], 32 * (i + 1))
                    for tt in range(TT):
                        dve.wait_ge(s_omm, START + 5 * n + tt + 1)
                        dve.wait_ge(s_x1, START + 5 * n + tt - 1)
                        ch.link(TT_(gated[(5 * s + tt) % 2], bank(tt), gate1[s][:, 0 if tt < 4 else 1, :], ALU.mult))
                        xs_ = x1[:, tt, bass.ds(n * BANK, BANK)]
                        TT_(xs_, xs_, gated[(5 * s + tt) % 2], ALU.add).then_inc(s_x1, 1)
            ch.passed(20)

            dve.wait_ge(s_n2rows, 2)
            for tt in range(TT):
                dve.wait_ge(s_ss2, START + 15 + tt + 1)
                dve.tensor_reduce(stat[:, tt, 0:1], ssq[:, tt, :], AX, ALU.add).then_inc(s_ssum, 1)
            def norm(tt):
                c = 0 if tt < 4 else 1
                dve.wait_ge(s_nroot, tt + 1)
                ch.link(dve.reciprocal(stat[:, tt, 1:2], stat[:, tt, 5:6]))
                if tt >= 2:
                    dve.wait_ge(s_h2out[tt % 2], 16 * (tt // 2))
                    dve.wait_ge(s_h2T, 4 * (tt - 1))
                STT(h2[tt % 2], x1[:, tt, :], stat[:, tt, 1:2], scale2[:, c, :], ALU.mult, ALU.mult).then_inc(s_h2m, 1)

            def route(tt):
                dve.wait_ge(s_logit, tt + 1)
                dve.tensor_reduce(stat[:, tt, 2:3], bank(4 + tt % 2, 16), AX, ALU.max, negate=True).then_inc(s_nmx, 1)
                dve.wait_ge(s_eaff, tt + 1)
                ch.link(dve.reciprocal(stat[:, tt, 4:5], stat[:, tt, 3:4]))
                TS_(aff[:, tt, :], aff[:, tt, :], stat[:, tt, 4:5], None, ALU.mult).then_inc(s_aff, 1)

            for tt in range(TT + 1):
                if tt < TT:
                    norm(tt)
                if tt >= 1:
                    route(tt - 1)
            dve.wait_ge(s_affT, 1)
            ch.mark(dve.tensor_copy(affT[:, 0:N_LAT].rearrange("p (r c) -> p r c", r=ROWS),
                                    bank(6)[0:EXPERTS, :].rearrange("p (c r) -> p r c", r=ROWS)))
            ch.link(dve.tensor_copy(affT[:, N_LAT:TOK], bank(7, P)[0:EXPERTS, :]))
            for vals, first, cap in ((affT[:, 0:N_LAT], 0, CAP_L), (affT[:, N_LAT:TOK], CAP_L, CAP_C)):
                for k in range(cap // 8):
                    eight = slice(first + 8 * k, first + 8 * k + 8)
                    ch.link(dve.max(top_v[:, eight], vals))
                    ch.link(dve.max_index(top_i[:, eight], top_v[:, eight], vals))
                    ch.link(dve.match_replace(vals, top_v[:, eight], vals, -1.0))
            lo, hi = top_a[:, 0:CAP_L], top_a[:, SLOTS:SLOTS + CAP_L]
            ch.mark(TS_(lo, top_i[:, 0:CAP_L], GRID_W - 1, 3, ALU.bitwise_and, ALU.logical_shift_left))
            ch.mark(TS_(hi, top_i[:, 0:CAP_L], 6, None, ALU.logical_shift_right))
            ch.link(dve.tensor_copy(top_f[:, CAP_L:SLOTS], top_i[:, CAP_L:SLOTS]))
            ch.mark(TS_(top_f[:, CAP_L:SLOTS], top_f[:, CAP_L:SLOTS], float(N_LAT), None, ALU.add))
            ch.link(TT_(lo, lo, hi, ALU.bitwise_or))
            dve.tensor_copy(top_f[:, 0:CAP_L], lo).then_inc(s_top, 1)
            dve.wait_ge(s_topT, 1)
            ch.mark(dve.tensor_copy(slot_gate, bank(0, 16)[0:SLOTS, :]))
            dve.tensor_copy(slot_row, bank(0, 16, 16)[0:SLOTS, :]).then_inc(s_slot, 1)
            ch.wait()
            dve.wait_ge(s_gate2, 32)

            def expert(e, s):
                for f in range(2):
                    dve.wait_ge(s_sg, 2 * e + f + 1)
                    dve.wait_ge(s_gu, START + 4 * e + 2 * f + 2)
                    dve.wait_ge(s_hhT, START + 2 * e)
                    cols = slice(f * BANK, (f + 1) * BANK)
                    TT_(act_h[:, cols], bank(2 * f + 1)[0:SLOTS, :], act_g[:, cols], ALU.mult).then_inc(s_hh, 1)
                dve.wait_ge(s_added, START + e)
                for j in range(4):
                    dve.wait_ge(s_dn, START + 4 * e + j + 1)
                    cols = slice(j * BANK, (j + 1) * BANK)
                    STT(y_e[s][:, cols], bank(6 + j % 2)[0:SLOTS, :], slot_gate[:, bass.ds(e, 1)], gate2[:, cols],
                        ALU.mult, ALU.mult).then_inc(s_ye, 1)

            with dve.Fori(0, EXPERTS // 2) as i:
                expert(2 * i, 0)
                expert(2 * i + 1, 1)

        @block.gpsimd
        def _(pool):
            ch = Chain(pool, s_pool)
            TT_ = pool.tensor_tensor
            pool.memset(mixT_[:, 4096:4096 + 2048], 0.0).then_inc(s_bzero, 1)
            pool.memset(cexp.rearrange("p c n -> p (c n)"), 0.0).then_inc(s_bzero, 1)

            def complex_product(re, im, a, b, scratch):
                t0, t1 = scratch
                ch.mark(TT_(t0, a[0], b[0], ALU.mult))
                ch.link(TT_(t1, a[1], b[1], ALU.mult))
                ch.link(TT_(re, t0, t1, ALU.subtract))
                ch.mark(TT_(t0, a[0], b[1], ALU.mult))
                ch.link(TT_(t1, a[1], b[0], ALU.mult))
                ch.link(TT_(im, t0, t1, ALU.add))

            pool.wait_ge(s_bload, 64)
            pool.wait_ge(s_pcol, 2)

            def spread(x):
                return x.rearrange("p (t n) -> p t n", t=32)

            f = [lanev[:, n, :].unsqueeze(2).to_broadcast([P, 32, 32]) for n in (3, 4)]
            complex_product(spread(bbar[:, 0]), spread(bbar[:, 1]), (spread(bexp[:, 0]), spread(bexp[:, 1])), f,
                            (spread(bscr[:, 0]), spread(bscr[:, 1])))
            pool.sem_inc(s_bbar, 1)
            for c in range(2):
                ch.link(pool.tensor_copy(E2[:, c, :, 0:1], lanev[:, 1 + c, :].unsqueeze(2)))

            k = 1
            while k < SEG:
                sc = [bscr[:, c, 0:32 * k].rearrange("p (t s) -> p t s", t=32) for c in range(2)]
                complex_product(E2[:, 0, :, k:2 * k], E2[:, 1, :, k:2 * k], (E2[:, 0, :, 0:k], E2[:, 1, :, 0:k]),
                                [E2[:, c, :, k - 1:k].to_broadcast([P, 32, k]) for c in range(2)], sc)
                k *= 2
            ch.mark(pool.memset(E1[:, 0, :, 0:1], 1.0))
            ch.mark(pool.memset(E1[:, 1, :, 0:1], 0.0))
            for c in range(2):
                ch.link(pool.tensor_copy(E1[:, c, :, 1:2], E2[:, c, :, SEG - 1:SEG]))
            k = 1
            while k < NSEG - 1:
                n = min(k, NSEG - 1 - k)
                sc = [bscr[:, c, 0:32 * n].rearrange("p (t s) -> p t s", t=32) for c in range(2)]
                complex_product(E1[:, 0, :, k + 1:k + 1 + n], E1[:, 1, :, k + 1:k + 1 + n],
                                (E1[:, 0, :, 1:1 + n], E1[:, 1, :, 1:1 + n]),
                                [E1[:, c, :, k:k + 1].to_broadcast([P, 32, n]) for c in range(2)], sc)
                k *= 2
            pool.sem_inc(s_tab, 1)

            def table(m, j):
                q, d = j // 2, j % 2
                turned = START + 8 * m + {0: -1, 1: 0, 2: -2}.get(j, j - 2)
                pool.wait_ge(s_back, turned)
                apart(pool)
                pool.wait_ge(s_backp, turned)
                apart(pool)
                R = rot[j % 3]
                e1 = [E1m[:, c, d, q, :].unsqueeze(2).to_broadcast([P, NSEG, SEG]) for c in range(2)]
                e2 = [E2m[:, c, d, q, :].unsqueeze(1).to_broadcast([P, NSEG, SEG]) for c in range(2)]

                def grid(x):
                    return x[:, 0:N_LAT].rearrange("p (a s) -> p a s", a=NSEG)

                ch.mark(TT_(grid(R[:, 0]), e1[0], e2[0], ALU.mult))
                ch.mark(TT_(grid(rot_tmp[:, 0]), e1[1], e2[1], ALU.mult))
                ch.mark(TT_(grid(R[:, 1]), e1[0], e2[1], ALU.mult))
                ch.link(TT_(grid(rot_tmp[:, 1]), e1[1], e2[0], ALU.mult))
                ch.mark(TT_(R[:, 0, 0:N_LAT], R[:, 0, 0:N_LAT], rot_tmp[:, 0], ALU.subtract))
                TT_(R[:, 1, 0:N_LAT], R[:, 1, 0:N_LAT], rot_tmp[:, 1], ALU.add).then_inc(s_table, 1)
                ch.wait()
                apart(pool)
                pool.wait_ge(s_table, 8 * m + j + 1)
                apart(pool)

            def add_parts(m, j):
                n = 8 * m + j
                pool.wait_ge(s_rmul, START + n + 1)
                apart(pool)
                pool.wait_ge(s_scan, START + n)
                apart(pool)
                pr = prod[j % 2]
                ch.mark(TT_(rin[:, 0], pr[:, 0], pr[:, 1], ALU.add))
                TT_(rin[:, 1], pr[:, 2], pr[:, 3], ALU.subtract).then_inc(s_radd, 1)

            def rotate_back(m, j):
                d = j % 2
                n = 8 * m + j
                pool.wait_ge(s_scan, START + n + 1)
                apart(pool)
                pool.wait_ge(s_y, START + n)
                apart(pool)
                pool.wait_ge(s_finm, START + n)
                apart(pool)
                parts = [(x, c, ph, sl) for x, c, ph in ((2, 1, 0), (3, 0, 1))
                         for sl in ((slice(0, TOK),) if d == 0 else (slice(0, N_LAT), slice(N_LAT, TOK)))]
                for x, c, ph, sl in parts:
                    dst = back[:, x, sl] if d == 0 else back[:, x, sl][:, ::-1]
                    last = TT_(dst, gsc[:, c, sl], rot[j % 3][:, ph, sl], ALU.mult)
                last.then_inc(s_backp, 1)

            with pool.Fori(0, CHUNKS_M) as m, ch.body(m, 8 * 6):
                pool.wait_ge(s_smcopy, 7 * (m + 1))
                apart(pool)
                table(m, 0)
                table(m, 1)
                for j in range(8):
                    add_parts(m, j)
                    if j < 6:
                        table(m, j + 2)
                    rotate_back(m, j)
            ch.passed(48 * CHUNKS_M)

            pool.wait_ge(s_span, 256)
            with pool.Fori(0, HEADS // 2) as i, ch.body(i, 6):
                for s in range(2):
                    h = 2 * i + s
                    pool.wait_ge(s_biasm, START + h)
                    apart(pool)
                    ch.link(pool.tensor_copy(span, spans[:, bass.ds(h, 1), :].rearrange("p h s -> p (h s)")))
                    pool.wait_ge(s_mx, START + 5 * h - 5)
                    apart(pool)
                    for v in range(3):
                        base = span[:, SPAN - 1 - BIAS_OFF[v]:SPAN - BIAS_OFF[v]]
                        view = bass.AP(base.tensor, base.offset, [list(base.ap[0]), [-1, 32], [-RPB_W, 8]])
                        last = TT_(biasm[s][:, v, :].rearrange("p (k i) -> p k i", i=8), view,
                                   masks[:, v, :].unsqueeze(2).to_broadcast([P, 32, 8]), ALU.add)
                        if v < 2:
                            ch.mark(last)
                    last.then_inc(s_biasm, 1)
            ch.passed(6 * HEADS // 2)

            pool.wait_ge(s_n2load, 96)
            for c in range(2):
                ch.link(TT_(scale2[:, c, :], scale2[:, c, :], norm2, ALU.mult))
                TT_(scale2[:, c, :], scale2[:, c, :], norm2, ALU.add).then_inc(s_n2rows, 1)
            for tt in range(TT):
                pool.wait_ge(s_h2m, tt + 1)
                apart(pool)
                TT_(h2[tt % 2], h2[tt % 2], shift2[:, 0 if tt < 4 else 1, :], ALU.add).then_inc(s_h2, 1)

            def gather(e, s):
                if not isinstance(e, int) or e > 1:
                    pool.wait_ge(s_scat, 16 * e - 16)
                    apart(pool)
                    pool.wait_ge(s_xsT, 4 * e - 4)
                    apart(pool)
                pool.tensor_copy(row_now[s], slot_row[:, bass.ds(e, 1)] if not isinstance(e, int) else
                                 slot_row[:, e:e + 1]).then_inc(s_row, 1)
                pool.wait_ge(s_row, e + 1)
                apart(pool)
                pool.indirect_dma_start(xs[s], None, h2_d, bass.IndirectOffsetOnAxis(ap=row_now[s], axis=0))\
                    .then_inc(s_gath[s], 16)

            def scatter(e, s):
                if not isinstance(e, int) or e > 0:
                    pool.wait_ge(s_scat, 16 * e)
                    apart(pool)
                pool.sem_inc(s_added, 1)
                pool.wait_ge(s_ye, START + 4 * e + 4)
                apart(pool)
                pool.indirect_dma_start(y_out, bass.IndirectOffsetOnAxis(ap=row_now[s], axis=0), y_e[s], None,
                                        compute_op=ALU.add).then_inc(s_scat, 16)

            pool.wait_ge(s_slot, 1)
            for s in range(2):
                pool.wait_ge(s_h2out[s], 16 * (3 - s))
            pool.wait_ge(s_logit, TT)
            gather(0, 0)
            gather(1, 1)
            pool.wait_ge(s_x1out, 16 * TT)
            scatter(0, 0)
            with pool.Fori(0, EXPERTS // 2 - 1) as i:
                gather(2 * i + 2, 0)
                scatter(2 * i + 1, 1)
                gather(2 * i + 3, 1)
                scatter(2 * i + 2, 0)
            scatter(EXPERTS - 1, 1)
            pool.wait_ge(s_scat, 16 * EXPERTS)


def kernel(**inputs):
    import numpy as _np
    import concourse.bacc as _bacc
    from concourse import mybir as _mybir
    from concourse.bass_utils import run_bass_kernel_spmd as _run

    a = {k: _np.asarray(v) for k, v in inputs.items()}
    lat = a["x_sample"][0].reshape(ROWS, GRID_W, D).transpose(1, 0, 2).reshape(N_LAT, D)
    q, k = _np.arange(16)[:, None], _np.arange(32)[None, :]
    first = [_np.maximum(q - 8, 0), q, _np.minimum(q + 8, 16)]
    mask = _np.stack([_np.where((k >= f) & (k < f + 16), 0.0, NEG) for f in first], 1)
    mask = _np.repeat(mask.reshape(16, 96), 8, axis=0)
    consts = _np.concatenate([_np.eye(P), _np.ones((P, P)), mask], axis=1).astype(_np.float32)
    arrays = {
        "x": _np.concatenate([lat, a["x_prompt"][0]], axis=0),
        "c_rows": _np.stack([a["c_ctx"], a["c"][0]]).reshape(32, P),
        "cache_k": a["cache_k"].reshape(P, D_ATTN), "cache_v": a["cache_v"].reshape(P, D_ATTN),
        "h0_re": a["state_ssm_re"].reshape(32, P), "h0_im": a["state_ssm_im"].reshape(32, P),
        "w_ada": a["w_ada"][0], "b_ada": a["b_ada"], "norm1": a["norm1_g"].reshape(16, P), "norm2": a["norm2_g"],
        "w_in": a["w_in"][0], "q_norm": a["q_norm_g"], "k_norm": a["k_norm_g"],
        "rpb": _np.pad(a["rel_pos_bias"][0, :, ::-1, ::-1].reshape(-1), RPB_PAD),
        "a_re": a["ssm_a_re"].reshape(32, P), "a_im": a["ssm_a_im"].reshape(32, P),
        "log_dt": a["ssm_log_dt"].reshape(32, 2),
        "b_re": a["ssm_b_re"].reshape(64, STATE, SSM_C), "b_im": a["ssm_b_im"].reshape(64, STATE, SSM_C),
        "c_re": a["ssm_c_re"].reshape(64, SSM_C, STATE), "c_im": a["ssm_c_im"].reshape(64, SSM_C, STATE),
        "ssm_d": a["ssm_d"].reshape(4, P), "w_glu": a["w_glu"][0], "b_glu": a["b_glu"].reshape(4, P),
        "w_out": a["w_out"][0], "w_router": a["w_router"][0],
        "w_gate": a["w_expert_gate"][0], "w_up": a["w_expert_up"][0], "w_down": a["w_expert_down"][0],
        "consts": consts,
    }
    nc = _bacc.Bacc("TRN2", target_bir_lowering=False, num_devices=1)
    arrays = {n: _np.ascontiguousarray(v) for n, v in arrays.items()}
    t = {n: nc.dram_tensor(f"in_{n}", v.shape, _mybir.dt.from_np(v.dtype), kind="ExternalInput").ap()
         for n, v in arrays.items()}
    shapes = {"y": (TOK, D), "new_k": (P, D_ATTN), "new_v": (P, D_ATTN), "st_re": (32, P), "st_im": (32, P)}
    out = {n: nc.dram_tensor(f"out_{n}", s, F32, kind="ExternalOutput").ap() for n, s in shapes.items()}
    trunk_step(nc, t, out)
    r = _run(nc, [{f"in_{n}": v for n, v in arrays.items()}], core_ids=[0]).results[0]
    y = r["out_y"]
    y_lat = y[0:N_LAT].reshape(GRID_W, ROWS, D).transpose(1, 0, 2).reshape(1, N_LAT, D)
    return (y[N_LAT:TOK].reshape(1, N_CTX, D), y_lat,
            r["out_new_k"].reshape(1, 1, N_CTX, HEADS, HD), r["out_new_v"].reshape(1, 1, N_CTX, HEADS, HD),
            r["out_st_re"].reshape(1, 1, 2, 32, STATE), r["out_st_im"].reshape(1, 1, 2, 32, STATE))
```
